# Optimizing a Trainium2 kernel written in Bass

```python
import jax, jax.numpy as jnp
from jax import lax
import numpy as np

D_MODEL = 1024
BATCH = 1
SEQ = 512
DEPTH = 1

CHUNK = 64
N_META = 16
HEAD_DIM = 64
N_HEADS = (D_MODEL // 2) // HEAD_DIM
N_KV_HEADS = 2
GQA_RATIO = N_HEADS // N_KV_HEADS
WINDOW = 128
WIN_CHUNKS = WINDOW // CHUNK
D_ATTN = N_HEADS * HEAD_DIM
D_KV = N_KV_HEADS * HEAD_DIM
POOL_WINDOWS = (2, 4, 8, 16)
N_POOL_GROUPS = len(POOL_WINDOWS)
D_POOL = D_MODEL // 2
POOL_GROUP_DIM = D_POOL // N_POOL_GROUPS
D_MIX = D_ATTN + D_POOL
D_IN = D_ATTN + 2 * D_KV + D_POOL
N_EXPERTS = 32
TOP_K = 4
D_EXPERT = D_MODEL
SWIGLU_LIMIT = 7.0
SWIGLU_ALPHA = 1.702
MOE_BLOCK = 256
EPS = 1e-5
NEG = -1e30

kernel_name = "hymba_swa_sink_pool_moe_streaming"

def rms_norm(x, g):
    xf = x.astype(jnp.float32)
    y = xf * lax.rsqrt(jnp.mean(xf * xf, axis=-1, keepdims=True) + EPS)
    return (y * g.astype(jnp.float32)).astype(x.dtype)

def sink_softmax(s, sink):
    m = jnp.maximum(jnp.max(s, axis=-1, keepdims=True), sink)
    e = jnp.exp(s - m)
    return e / (jnp.sum(e, axis=-1, keepdims=True) + jnp.exp(sink - m))

def window_attention(q, k, v, sinks):
    B, L = q.shape[0], q.shape[1]
    S = L - N_META
    NC = S // CHUNK
    scale = HEAD_DIM ** -0.5
    qm = q[:, :N_META].reshape(B, N_META, N_KV_HEADS, GQA_RATIO, HEAD_DIM)
    km, vm = k[:, :N_META], v[:, :N_META]
    qr = q[:, N_META:].reshape(B, NC, CHUNK, N_KV_HEADS, GQA_RATIO, HEAD_DIM)
    kr = k[:, N_META:].reshape(B, NC, CHUNK, N_KV_HEADS, HEAD_DIM)
    vr = v[:, N_META:].reshape(B, NC, CHUNK, N_KV_HEADS, HEAD_DIM)
    offsets = list(range(WIN_CHUNKS - 1, -1, -1))

    def band(t):
        parts = [jnp.pad(t, ((0, 0), (j, 0), (0, 0), (0, 0), (0, 0)))[:, :NC] for j in offsets]
        return jnp.concatenate(parts, axis=2)

    kb, vb = band(kr), band(vr)
    band_valid = (jnp.arange(NC)[:, None] - jnp.asarray(offsets)[None, :]) >= 0
    band_valid = jnp.repeat(band_valid, CHUNK, axis=1)
    valid = jnp.concatenate([jnp.ones((NC, N_META), bool), band_valid], axis=1)

    s_meta = jnp.einsum('bnqgrd,bkgd->bngrqk', qr, km).astype(jnp.float32)
    s_band = jnp.einsum('bnqgrd,bnkgd->bngrqk', qr, kb).astype(jnp.float32)
    s = jnp.concatenate([s_meta, s_band], axis=-1) * scale
    s = jnp.where(valid[None, :, None, None, None, :], s, NEG)
    sink = sinks.astype(jnp.float32).reshape(N_KV_HEADS, GQA_RATIO)
    p = sink_softmax(s, sink[None, None, :, :, None, None]).astype(v.dtype)
    o = (jnp.einsum('bngrqk,bkgd->bnqgrd', p[..., :N_META], vm)
         + jnp.einsum('bngrqk,bnkgd->bnqgrd', p[..., N_META:], vb))
    o = o.reshape(B, S, D_ATTN)

    s_mm = jnp.einsum('bqgrd,bkgd->bgrqk', qm, km).astype(jnp.float32) * scale
    p_mm = sink_softmax(s_mm, sink[None, :, :, None, None]).astype(v.dtype)
    o_m = jnp.einsum('bgrqk,bkgd->bqgrd', p_mm, vm).reshape(B, N_META, D_ATTN)
    return jnp.concatenate([o_m, o], axis=1)

def multiscale_pool(u, w_pool, pool_scale):
    B, L, _ = u.shape
    uf = u.astype(jnp.float32)
    cs = jnp.pad(jnp.cumsum(uf, axis=1), ((0, 0), (1, 0), (0, 0)))
    pos = jnp.arange(L, dtype=jnp.float32)
    outs = []
    for g, w in enumerate(POOL_WINDOWS):
        sl = slice(g * POOL_GROUP_DIM, (g + 1) * POOL_GROUP_DIM)
        c = cs[..., sl]
        lagged = jnp.pad(c[:, :L + 1 - w], ((0, 0), (w - 1, 0), (0, 0)))
        count = jnp.minimum(pos + 1.0, float(w))[None, :, None]
        outs.append((c[:, 1:] - lagged) / count - uf[..., sl])
    d = jnp.stack(outs, axis=2).astype(u.dtype)
    y = jnp.einsum('blgc,gce->blge', d, w_pool).reshape(B, L, D_POOL)
    return y * pool_scale

def moe_ffn(h, w_router, b_router, w_gate, b_gate, w_up, b_up, w_down, b_down):
    N, D = h.shape
    logits = jnp.matmul(h, w_router).astype(jnp.float32) + b_router.astype(jnp.float32)
    top_logit, top_idx = lax.top_k(logits, TOP_K)
    gates = jax.nn.softmax(top_logit, axis=-1)
    A = N * TOP_K
    flat_e = top_idx.reshape(A).astype(jnp.int32)
    flat_tok = jnp.arange(A, dtype=jnp.int32) // TOP_K
    flat_g = gates.reshape(A)
    order = jnp.argsort(flat_e)
    e_sorted = flat_e[order]
    counts = jnp.bincount(flat_e, length=N_EXPERTS).astype(jnp.int32)
    padded = ((counts + MOE_BLOCK - 1) // MOE_BLOCK) * MOE_BLOCK
    start_sorted = jnp.cumsum(counts) - counts
    pad_end = jnp.cumsum(padded)
    start_pad = pad_end - padded
    rank = jnp.arange(A, dtype=jnp.int32) - start_sorted[e_sorted]
    dest = start_pad[e_sorted] + rank
    n_blocks = (A + N_EXPERTS * (MOE_BLOCK - 1) + MOE_BLOCK - 1) // MOE_BLOCK
    P = n_blocks * MOE_BLOCK
    tok_buf = jnp.full((P,), N, jnp.int32).at[dest].set(flat_tok[order])
    gate_buf = jnp.zeros((P,), jnp.float32).at[dest].set(flat_g[order])
    block_expert = jnp.minimum(
        jnp.searchsorted(pad_end, jnp.arange(n_blocks, dtype=jnp.int32) * MOE_BLOCK, side='right'),
        N_EXPERTS - 1).astype(jnp.int32)
    h_pad = jnp.concatenate([h, jnp.zeros((1, D), h.dtype)], axis=0)

    def expert_block(args):
        toks, e = args
        xb = h_pad[toks]
        gate = jnp.minimum(xb @ w_gate[e] + b_gate[e], SWIGLU_LIMIT)
        up = jnp.clip(xb @ w_up[e] + b_up[e], -SWIGLU_LIMIT, SWIGLU_LIMIT)
        glu = gate * jax.nn.sigmoid(SWIGLU_ALPHA * gate)
        return ((up + 1.0) * glu) @ w_down[e] + b_down[e]

    y_buf = lax.map(expert_block, (tok_buf.reshape(n_blocks, MOE_BLOCK), block_expert))
    y_buf = y_buf.reshape(P, D) * gate_buf[:, None].astype(h.dtype)
    return jax.ops.segment_sum(y_buf, tok_buf, num_segments=N + 1)[:N]

def setup_inputs(seed: int = 0) -> dict:
    key = jax.random.key(seed)
    ks = jax.random.split(key, 20)
    f32 = jnp.float32
    nrm = lambda k, shape, s: (jax.random.normal(k, shape, f32) * s).astype(f32)
    return {
        "x": nrm(ks[0], (BATCH, SEQ, D_MODEL), 1.0),
        "meta_tokens": nrm(ks[1], (N_META, D_MODEL), 1.0),
        "norm_mix_g": 1.0 + nrm(ks[2], (DEPTH, D_MODEL), 0.02),
        "w_in": nrm(ks[3], (DEPTH, D_MODEL, D_IN), D_MODEL ** -0.5),
        "b_in": nrm(ks[4], (DEPTH, D_IN), 0.02),
        "attn_sinks": nrm(ks[5], (DEPTH, N_HEADS), 0.5),
        "w_pool": nrm(ks[6], (DEPTH, N_POOL_GROUPS, POOL_GROUP_DIM, POOL_GROUP_DIM), POOL_GROUP_DIM ** -0.5),
        "pool_scale": 1.0 + nrm(ks[7], (DEPTH, D_POOL), 0.02),
        "w_out": nrm(ks[8], (DEPTH, D_MIX, D_MODEL), D_MIX ** -0.5),
        "norm_ffn_g": 1.0 + nrm(ks[9], (DEPTH, D_MODEL), 0.02),
        "w_router": nrm(ks[10], (DEPTH, D_MODEL, N_EXPERTS), D_MODEL ** -0.5),
        "b_router": nrm(ks[11], (DEPTH, N_EXPERTS), 0.01),
        "w_gate": nrm(ks[12], (DEPTH, N_EXPERTS, D_MODEL, D_EXPERT), D_MODEL ** -0.5),
        "b_gate": nrm(ks[13], (DEPTH, N_EXPERTS, D_EXPERT), 0.02),
        "w_up": nrm(ks[14], (DEPTH, N_EXPERTS, D_MODEL, D_EXPERT), D_MODEL ** -0.5),
        "b_up": nrm(ks[15], (DEPTH, N_EXPERTS, D_EXPERT), 0.02),
        "w_down": nrm(ks[16], (DEPTH, N_EXPERTS, D_EXPERT, D_MODEL), D_EXPERT ** -0.5),
        "b_down": nrm(ks[17], (DEPTH, N_EXPERTS, D_MODEL), 0.02),
        "norm_final_g": 1.0 + nrm(ks[18], (D_MODEL,), 0.02),
    }

def reference(x, meta_tokens, norm_mix_g, w_in, b_in, attn_sinks, w_pool, pool_scale, w_out,
              norm_ffn_g, w_router, b_router, w_gate, b_gate, w_up, b_up, w_down, b_down,
              norm_final_g):
    B = x.shape[0]
    meta = jnp.broadcast_to(meta_tokens[None].astype(x.dtype), (B, N_META, D_MODEL))
    h = jnp.concatenate([meta, x], axis=1)
    L = h.shape[1]
    for l in range(DEPTH):
        u = rms_norm(h, norm_mix_g[l])
        proj = jnp.matmul(u, w_in[l]) + b_in[l]
        q = proj[..., :D_ATTN].reshape(B, L, N_HEADS, HEAD_DIM)
        k = proj[..., D_ATTN:D_ATTN + D_KV].reshape(B, L, N_KV_HEADS, HEAD_DIM)
        v = proj[..., D_ATTN + D_KV:D_ATTN + 2 * D_KV].reshape(B, L, N_KV_HEADS, HEAD_DIM)
        p_in = proj[..., D_ATTN + 2 * D_KV:]
        a = window_attention(q, k, v, attn_sinks[l])
        pm = multiscale_pool(p_in, w_pool[l], pool_scale[l])
        mix = jnp.concatenate([a, pm], axis=-1)
        h = h + jnp.matmul(mix, w_out[l])
        f = rms_norm(h, norm_ffn_g[l]).reshape(B * L, D_MODEL)
        y = moe_ffn(f, w_router[l], b_router[l], w_gate[l], b_gate[l], w_up[l], b_up[l],
                    w_down[l], b_down[l])
        h = h + y.reshape(B, L, D_MODEL)
    out = rms_norm(h, norm_final_g)
    return out[:, N_META:]


_drawn_inputs = setup_inputs


def setup_inputs(seed=0):
    import zlib

    import numpy as np

    out = dict(_drawn_inputs(seed))
    spreads = {}
    factors = {'attn_sinks': 6.04, 'b_gate': 7.062, 'b_up': 8.0, 'b_down': 6.756, 'norm_final_g': 2.907}
    for name, (base, spread) in spreads.items():
        noise = np.random.default_rng([zlib.crc32(name.encode()), seed]).standard_normal(out[name].shape)
        drawn = base * np.exp(spread * noise) if base else spread * noise
        out[name] = __import__('jax').numpy.asarray(drawn.astype(out[name].dtype))
    for name, factor in factors.items():
        out[name] = (out[name] * factor).astype(out[name].dtype)
    return out
```

```python
from contextlib import ExitStack

import concourse.bass as bass
from concourse import mybir

F32 = mybir.dt.float32
BF16 = mybir.dt.bfloat16
U32 = mybir.dt.uint32
I32 = mybir.dt.int32
ALU = mybir.AluOpType
ACT = mybir.ActivationFunctionType
AX = mybir.AxisListType

P = 128
D = 1024
KC = D // P
SEQ = 512
NT = SEQ // P
META = 16
HD = 64
SCALE = HD ** -0.5
HEADS = 8
HALF = HEADS // 2
PREV = 64 + META
KEYS = PREV + P
NG = 4
POOL_WINDOWS = (2, 4, 8, 16)
NE = 32
TOPK = 4
CAP = 96
ROUNDS = -(-SEQ // CAP)
LIMIT, ALPHA = 7.0, 1.702
EPS = 1e-5
NEG = -1e30
FAR = 1.0e6
UNROLL = 4
BODIES = NE // UNROLL
UNITS = 6
SLOTS = 8
COLS = 512
AHEAD = 2
NEP = NE + AHEAD
FIRST_SUMS = 32


def build(nc, a, out):
    ctx = ExitStack()
    with ctx:
        def sb(name, shape, dt=F32):
            return ctx.enter_context(nc.sbuf_tensor(name, shape, dt))

        def sem(name):
            return ctx.enter_context(nc.semaphore(name))

        normed_rows = nc.dram_tensor("normed_rows", (SEQ, D), F32).ap()
        sums = nc.dram_tensor("sums", (SEQ + CAP, D), F32).ap()

        ring = [sb(f"ring{i}", [P, KC * COLS]) for i in range(SLOTS)]
        slot = [r[:].rearrange("p (k n) -> p k n", k=KC) for r in ring]
        uT = ring[0][:].rearrange("p (k n) -> p k n", k=KC)
        qT = ring[1][:, 0:4 * SEQ].rearrange("p (c n) -> p c n", c=4)
        diffT = ring[1][:, 4 * SEQ:8 * SEQ].rearrange("p (c n) -> p c n", c=4)
        probs = ring[2][:, 0:HEADS * KEYS].rearrange("p (h k) -> p h k", h=HEADS)
        o = HEADS * KEYS
        probsT_prev = ring[2][0:PREV, o:o + 512].rearrange("p (h q) -> p h q", h=4)
        probsT_own = ring[2][:, o + 512:o + 1024].rearrange("p (h q) -> p h q", h=4)
        o += 1024
        L = META + SEQ
        wsum = [ring[2][:, o + i * L:o + (i + 1) * L] for i in range(2)]
        wq, wp = slot[3], slot[4]
        wkv = ring[5][:, 0:KC * 256].rearrange("p (k n) -> p k n", k=KC)
        o = KC * 256
        kT = ring[5][:, o:o + SEQ]
        o += SEQ
        k_prev = ring[5][:, o:o + NT * PREV].rearrange("p (m k) -> p m k", m=NT)
        o += NT * PREV
        v_own = ring[5][:, o:o + NT * P].rearrange("p (m n) -> p m n", m=NT)
        o += NT * P
        v_prev = ring[5][:, o:o + NT * P].rearrange("p (m n) -> p m n", m=NT)
        wout = [slot[6], slot[7]]

        hx = sb("hx", [P, NT, D])
        work = sb("work", [P, 3 * KC * SEQ])
        third = [work[:, i * KC * SEQ:(i + 1) * KC * SEQ] for i in range(3)]
        xn = third[0].rearrange("p (t d) -> p t d", t=NT)
        mixT = third[0].rearrange("p (k n) -> p k n", k=KC)
        normed = third[1].rearrange("p (t d) -> p t d", t=NT)
        pT = third[1][:, 0:NG * L].rearrange("p (g n) -> p g n", g=NG)
        meta_x = third[1][0:META, NG * L:NG * L + D]
        bias_rows = third[2][:, 0:6 * P].rearrange("p (b h n) -> p b h n", b=3, h=2)
        meta_n = third[2][0:META, 6 * P:6 * P + D]
        fT = third[2].rearrange("p (k n) -> p k n", k=KC)
        o = 0

        def carve(n):
            nonlocal o
            o += n
            return work[:, o - n:o]

        x_rows = [carve(D)[0:CAP] for _ in range(2)]
        xT = [carve(KC * CAP).rearrange("p (k n) -> p k n", k=KC) for _ in range(2)]
        gate_t = carve(KC * CAP).rearrange("p (k n) -> p k n", k=KC)
        glu_t = carve(KC * CAP).rearrange("p (k n) -> p k n", k=KC)
        up_t = carve(KC * CAP).rearrange("p (k n) -> p k n", k=KC)
        act_t = carve(KC * CAP).rearrange("p (k n) -> p k n", k=KC)
        yT = carve(KC * CAP).rearrange("p (k n) -> p k n", k=KC)
        y_rows = [carve(D)[0:CAP] for _ in range(2)]
        hot = carve(NT * CAP).rearrange("p (t n) -> p t n", t=NT)
        g_final = carve(D)

        ident = sb("ident", [P, P])
        iota_cap = sb("iota_cap", [P, CAP])
        iota_exp = sb("iota_exp", [P, NE])
        steps = sb("steps", [P, ROUNDS])
        earlier = sb("earlier", [P, P], BF16)
        ones = sb("ones", [P, P], BF16)
        block_of = sb("block_of", [P, P], BF16)
        unseen = sb("unseen", [P, 2, KEYS], BF16)
        pace = sb("pace", [1, 2 * UNROLL])
        zeros = sb("zeros", [CAP, D // 4])
        spare = sb("spare", [P, 2])
        place_in = sb("place_in", [P, NT, 3])
        vec_rows = third[2][0:32, 6 * P + D:7 * P + D]
        vec = sb("vec", [P, 32])
        VG_MIX, VG_FFN, VB_Q, VB_K, VB_P, V_SCALE = 0, 8, 16, 20, 21, 25
        bv = ring[2][:, 4096 - P:4096]
        sinks = sb("sinks", [P, HEADS])
        b_router = sb("b_router", [P, NE])
        w_router = sb("w_router", [P, KC, NE])
        w_pool = sb("w_pool", [P, NG, P])
        uT_meta = sb("uT_meta", [P, KC, META])
        sq = sb("sq", [P, 5])
        rstd = sb("rstd", [P, 5])
        mx = sb("mx", [P, HEADS])
        negm = sb("negm", [P, HEADS])
        sink_e = sb("sink_e", [P, HEADS])
        den = sb("den", [P, HEADS])
        logits = sb("logits", [P, NT, NE])
        top = sb("top", [P, NT, 8])
        top_at = sb("top_at", [P, NT, 8], U32)
        top_f = sb("top_f", [P, NT, 8])
        top_e = sb("top_e", [P, NT, TOPK])
        top_s = sb("top_s", [P, NT])
        chosen = sb("chosen", [P, TOPK, NE])
        chosen_g = sb("chosen_g", [P, TOPK, NE])
        mask = sb("mask", [P, NT, NE])
        mask_b = sb("mask_b", [P, NT, NE], BF16)
        ranks = sb("ranks", [P, NT, NEP])
        gates = sb("gates", [P, NT, NEP])
        count = sb("count", [P, 1])
        over = sb("over", [P, ROUNDS])
        rounds_f = sb("rounds_f", [P, 1])
        rounds_i = sb("rounds_i", [P, 1], I32)
        bias = sb("bias", [P, 3, (NE + 1) * KC])
        bias_e = sb("bias_e", [P, 2, 3, KC])
        from_row = sb("from_row", [P, UNROLL], U32)
        to_row = sb("to_row", [P, UNROLL], U32)
        to_f = sb("to_f", [P, 1])
        gate_c = sb("gate_c", [P, UNROLL])

        bank = [ctx.enter_context(nc.psum_tensor(f"bank{i}", [P, 512], F32)) for i in range(8)]

        x_in = [sem(f"x_in{t}") for t in range(NT)]
        meta_in, vec_in, consts_in = sem("meta_in"), sem("vec_in"), sem("consts_in")
        wkv_in, wq_in, wp_in, wout_in = sem("wkv_in"), sem("wq_in"), sem("wp_in"), sem("wout_in")
        weights_in = [sem(f"weights_in{i}") for i in range(SLOTS)]
        consts_set = sem("consts_set")
        squared, rooted, var_set, xn_set = sem("squared"), sem("rooted"), sem("var_set"), sem("xn_set")
        vecs_T, vecs_set = sem("vecs_T"), sem("vecs_set")
        u_T, u_set = sem("u_T"), sem("u_set")
        proj, proj_set = sem("proj"), sem("proj_set")
        v_set = sem("v_set")
        scored, max_set, exp_set, probs_set = sem("scored"), sem("max_set"), sem("exp_set"), sem("probs_set")
        probs_T, probsT_set = sem("probs_T"), sem("probsT_set")
        attended, mix_set = sem("attended"), sem("mix_set")
        diff_set, pooled, pooled_set = sem("diff_set"), sem("pooled"), sem("pooled_set")
        p_set = sem("p_set")
        mixed, h_set, f_T, f_set, routed, logits_set = (
            sem("mixed"), sem("h_set"), sem("f_T"), sem("f_set"), sem("routed"), sem("logits_set"))
        top_set, top_exp = sem("top_set"), sem("top_exp")
        mask_set, ranked, rounds_set = sem("mask_set"), sem("ranked"), sem("rounds_set")
        normed_stored = sem("normed_stored")
        sums_set = sem("sums_set")
        g_final_in = sem("g_final_in")
        dve_seq = sem("dve_seq")
        ranks_moved, hot_set, place_ready, place_set = (
            sem("ranks_moved"), sem("hot_set"), sem("place_ready"), sem("place_set"))
        gathered = [sem(f"gathered{i}") for i in range(2)]
        x_T, xT_set, bias_set = sem("x_T"), sem("xT_set"), sem("bias_set")
        gate_ready, gate_capped, sigmoids = sem("gate_ready"), sem("gate_capped"), sem("sigmoids")
        up_ready, up_capped, glu_set, act_set = sem("up_ready"), sem("up_capped"), sem("glu_set"), sem("act_set")
        down_ready, y_biased, y_T, y_scaled = sem("down_ready"), sem("y_biased"), sem("y_T"), sem("y_scaled")
        sums_landed = sem("sums_landed")
        final_in = [sem(f"final_in{t}") for t in range(NT)]
        out_set, stored = sem("out_set"), sem("stored")

        def col(v, n):
            return vec[:, v:v + n]

        def spread(ap, n):
            return ap.unsqueeze(2).to_broadcast([ap.shape[0], ap.shape[1], n])

        weight = [a["w_gate"], a["w_up"], a["w_gate"], a["w_up"], a["w_down"], a["w_down"]]
        which_half = [0, 0, 1, 1, 0, 1]

        def unit_src(at, u):
            c = which_half[u] * COLS
            whole = weight[u][0].rearrange("e d n -> (e d n)")
            return whole[bass.ds(at, D * D)].rearrange("(k p n) -> p k n", p=P, n=D)[:, :, c:c + COLS]

        def slot_of(j, u):
            return (UNITS * j + u) % SLOTS

        block = ctx.enter_context(nc.Block())

        @block.sync
        def _(sp):
            xr = a["x"][0].rearrange("(t p) d -> p t d", p=P)
            for t in range(NT):
                sp.dma_start(hx[:, t, :], xr[:, t, :]).then_inc(x_in[t], 16)
            sp.dma_start(meta_x, a["meta_tokens"]).then_inc(meta_in, 16)
            w_in = a["w_in"][0].rearrange("(k p) n -> p k n", p=P)
            sp.dma_start(wkv, w_in[:, :, 512:768]).then_inc(wkv_in, 16)
            sp.dma_start(wq, w_in[:, :, 0:512]).then_inc(wq_in, 16)
            sp.dma_start(wp, w_in[:, :, 768:1280]).then_inc(wp_in, 16)
            w_out = a["w_out"][0].rearrange("(k p) n -> p k n", p=P)
            for h in range(2):
                sp.dma_start(wout[h], w_out[:, :, h * COLS:(h + 1) * COLS]).then_inc(wout_in, 16)

            start = sp.alloc_register("unit_start")

            def load(e, j, u, wait=None):
                if wait:
                    sp.reg_mul(start, e, D * D)
                    sp.reg_sub(start, start, COLS)
                    at = sp.snap(start, min_val=D * D - COLS, max_val=(NE - 1) * D * D - COLS) + COLS
                    freed(*wait)
                else:
                    at = e * D * D
                sp.dma_start(slot[slot_of(j, u)], unit_src(at, u)).then_inc(weights_in[slot_of(j, u)], 16)

            for n in range(SLOTS):
                if n == 0:
                    sp.wait_ge(proj, 7 + NG)
                if n == 1:
                    sp.wait_ge(pooled, NG)
                if n == 6:
                    sp.wait_ge(mixed, NT)
                load(n // UNITS, n // UNITS, n % UNITS)

            def freed(u, A):
                if u == 4 or u == 5:
                    sp.wait_ge(down_ready, A * 2 + (u - 3))
                else:
                    sp.wait_ge(gate_ready if u % 2 == 0 else up_ready, A * 8 + 4 * (1 + u // 2))

            sp.wait_ge(rounds_set, 1)
            rounds = sp.value_load(rounds_i[0:1, 0:1], min_val=1, max_val=ROUNDS)
            sp.dma_start(g_final, a["norm_final_g"].partition_broadcast(P)).then_inc(g_final_in, 16)
            with sp.Fori(0, rounds) as r:
                with sp.Fori(0, BODIES - 1) as b:
                    for n in range(UNROLL * UNITS):
                        j, u = divmod(n, UNITS)
                        j2, u2 = divmod(n + SLOTS, UNITS)
                        load(b * UNROLL + j2, j2, u2, (u, r * NE + b * UNROLL + j))
                for n in range(UNROLL * UNITS - SLOTS):
                    j, u = divmod(n, UNITS)
                    j2, u2 = divmod(n + SLOTS, UNITS)
                    freed(u, r * NE + (NE - UNROLL + j))
                    load(NE - UNROLL + j2, j2, u2)
                with sp.If(r + 1 < rounds):
                    for n in range(SLOTS):
                        j, u = divmod(n + UNROLL * UNITS - SLOTS, UNITS)
                        freed(u, r * NE + (NE - UNROLL + j))
                        load(n // UNITS, n // UNITS, n % UNITS)

            sp.wait_ge(sums_landed, rounds * (16 * NE) + FIRST_SUMS)
            sr = sums[0:SEQ, :].rearrange("(t p) d -> p t d", p=P)
            for t in range(NT):
                sp.dma_start(hx[:, t, :], sr[:, t, :]).then_inc(final_in[t], 16)
            outr = out[0].rearrange("(t p) d -> p t d", p=P)
            for t in range(NT):
                sp.wait_ge(out_set, t + 1)
                sp.dma_start(outr[:, t, :], normed[:, t, :]).then_inc(stored, 16)
            sp.wait_ge(stored, 16 * NT)

        @block.gpsimd
        def _(pool):
            g = nc.gpsimd
            g.memset(ident[:], 0.0).then_inc(consts_set, 1)
            pool.wait_ge(consts_set, 1)
            g.affine_select(out=ident[:], in_=ident[:], compare_op=ALU.not_equal, fill=1.0, base=0,
                            pattern=[[-1, P]], channel_multiplier=1).then_inc(consts_set, 1)
            g.memset(earlier[:], 1.0).then_inc(consts_set, 1)
            pool.wait_ge(consts_set, 3)
            g.affine_select(out=earlier[:], in_=earlier[:], compare_op=ALU.is_gt, fill=0.0, base=0,
                            pattern=[[1, P]], channel_multiplier=-1)
            g.memset(ones[:], 1.0)
            g.memset(zeros[:], 0.0)
            g.iota(iota_cap[:], pattern=[[1, CAP]], base=0, channel_multiplier=0, allow_small_or_imprecise_dtypes=True)
            g.iota(iota_exp[:], pattern=[[1, NE]], base=0, channel_multiplier=0, allow_small_or_imprecise_dtypes=True)
            g.iota(steps[:], pattern=[[CAP, ROUNDS]], base=0, channel_multiplier=0, allow_small_or_imprecise_dtypes=True)
            g.iota(spare[:, 0:1], pattern=[[1, 1]], base=SEQ, channel_multiplier=1, allow_small_or_imprecise_dtypes=True)
            g.iota(spare[:, 1:2], pattern=[[1, 1]], base=-SEQ, channel_multiplier=-1, allow_small_or_imprecise_dtypes=True)
            g.memset(place_in[:], 1.0).then_inc(consts_set, 1)
            pool.wait_ge(consts_set, 4)
            g.iota(place_in[:, :, 0:1], pattern=[[P, NT], [0, 1]], base=0, channel_multiplier=1,
                   allow_small_or_imprecise_dtypes=True)
            g.memset(ranks[:], -FAR)
            g.memset(gates[:], 0.0)
            g.memset(bias[:, :, NE * KC:(NE + 1) * KC], 0.0).then_inc(consts_set, 1)

            pool.wait_ge(consts_set, 5)
            for c in range(2):
                pool.dma_start(sums[SEQ:SEQ + CAP, c * (D // 2):(c + 1) * (D // 2)].rearrange("p (c n) -> p c n", c=2),
                               zeros[:].unsqueeze(1).to_broadcast([CAP, 2, D // 4])).then_inc(sums_landed, 16)

            pool.wait_ge(rounds_set, 1)
            rounds = pool.value_load(rounds_i[0:1, 0:1], min_val=1, max_val=ROUNDS)

            pool.wait_ge(normed_stored, 16)
            pool.wait_ge(sums_set, 16)

            def pace_step(i):
                g.tensor_tensor(pace[0:1, i:i + 1], steps[0:1, 0:1], steps[0:1, 0:1], ALU.add)

            def gather(j, I):
                pool.wait_ge(place_set, I + 1)
                pace_step(j % UNROLL)
                g.indirect_dma_start(out=x_rows[j % 2], out_offset=None, in_=normed_rows,
                                     in_offset=bass.IndirectOffsetOnAxis(ap=from_row[0:CAP, j % UNROLL:j % UNROLL + 1],
                                                                         axis=0)
                                     ).then_inc(gathered[j % 2], 16)

            def stage_bias(e, j):
                g.tensor_copy(bias_e[:, j % 2], bias[:, :, bass.ds(e * KC, KC)]).then_inc(bias_set, 1)

            with pool.Fori(0, rounds) as r:
                gather(0, r * NEP)
                stage_bias(0, 0)
                gather(1, r * NEP + 1)
                with pool.Fori(0, BODIES) as b:
                    for j in range(UNROLL):
                        gather(j + AHEAD, r * NEP + b * UNROLL + (j + AHEAD))
                        stage_bias(b * UNROLL + (j + 1), j + 1)
                        A = r * NE + b * UNROLL + j
                        pool.wait_ge(y_scaled, A * 2 + 3)
                        pool.wait_ge(sums_landed, A * 16 + FIRST_SUMS)
                        pace_step(UNROLL + j)
                        g.indirect_dma_start(out=sums, out_offset=bass.IndirectOffsetOnAxis(
                                                 ap=to_row[0:CAP, j:j + 1], axis=0),
                                             in_=y_rows[j % 2], in_offset=None,
                                             compute_op=ALU.add).then_inc(sums_landed, 16)

        @block.scalar
        def _(act):
            s = nc.scalar
            b_in = a["b_in"][0]
            for row, n, src in (
                    (VG_MIX, 8, a["norm_mix_g"][0].rearrange("(k p) -> k p", p=P)),
                    (VG_FFN, 8, a["norm_ffn_g"][0].rearrange("(k p) -> k p", p=P)),
                    (VB_Q, 5, b_in[0:640].rearrange("(k p) -> k p", p=P)),
                    (VB_P, 4, b_in[768:1280].rearrange("(k p) -> k p", p=P)),
                    (V_SCALE, 4, a["pool_scale"][0].rearrange("(k p) -> k p", p=P))):
                act.dma_start(vec_rows[row:row + n, :], src).then_inc(vec_in, 16)
            for i, name in enumerate(("b_gate", "b_up", "b_down")):
                for h in range(2):
                    act.dma_start(bias_rows[:, i, h, :],
                                  a[name][0].rearrange("e (k p) -> (e k) p", p=P)[h * P:(h + 1) * P, :]
                                  ).then_inc(vec_in, 16)
            act.dma_start(bv[:], b_in[640:768].partition_broadcast(P)).then_inc(consts_in, 16)
            act.dma_start(sinks[:], a["attn_sinks"][0].partition_broadcast(P)).then_inc(consts_in, 16)
            act.dma_start(b_router[:], a["b_router"][0].partition_broadcast(P)).then_inc(consts_in, 16)
            act.dma_start(w_router[:], a["w_router"][0].rearrange("(k p) n -> p k n", p=P)).then_inc(consts_in, 16)
            act.dma_start(w_pool[:], a["w_pool"][0].rearrange("g c e -> c g e")).then_inc(consts_in, 16)

            for t in range(NT + 1):
                n = P if t < NT else META
                if t < NT:
                    act.wait_ge(x_in[t], 16)
                    s.activation(xn[:, t, :], hx[:, t, :], ACT.Square, accum_out=sq[:, t:t + 1]).then_inc(squared, 1)
                else:
                    act.wait_ge(meta_in, 16)
                    s.activation(meta_n, meta_x, ACT.Square, accum_out=sq[0:META, t:t + 1]).then_inc(squared, 1)
                act.wait_ge(var_set, t + 1)
                s.activation(rstd[0:n, t:t + 1], rstd[0:n, t:t + 1], ACT.Sqrt).then_inc(rooted, 1)

            act.wait_ge(vecs_set, 1)
            act.wait_ge(proj, 1)
            s.activation(kT, bank[0][:, 0:SEQ], ACT.Identity, bias=col(VB_K, 1)).then_inc(proj_set, 1)
            act.wait_ge(proj, 2)
            s.activation(k_prev[:, 0, 64:PREV], bank[5][:, 0:META], ACT.Identity, bias=col(VB_K, 1))
            for c in range(NG):
                i = s.activation(pT[:, c, 0:META], bank[5][:, META * (1 + c):META * (2 + c)], ACT.Identity,
                                 bias=col(VB_P + c, 1))
            i.then_inc(proj_set, 1)
            for c in range(4):
                act.wait_ge(proj, 4 + c)
                s.activation(qT[:, c, :], bank[1 + c][:], ACT.Identity, bias=col(VB_Q + c, 1)).then_inc(proj_set, 1)

            for m in range(NT):
                act.wait_ge(max_set, m + 1)
                for h in range(HEADS):
                    s.activation(probs[:, h, :], bank[h // 2][:, (h % 2) * KEYS:(h % 2 + 1) * KEYS], ACT.Exp,
                                 bias=negm[:, h:h + 1], scale=SCALE, accum_out=den[:, h:h + 1])
                s.activation(sink_e[:], sink_e[:], ACT.Exp).then_inc(exp_set, 1)
                act.wait_ge(proj, 8 + m)
                s.activation(pT[:, m, META:], bank[4][:], ACT.Identity, bias=col(VB_P + m, 1)).then_inc(p_set, 1)
                for g in range(2):
                    act.wait_ge(probs_T, 2 * m + g + 1)
                    s.activation(probsT_own, bank[6 if g == 0 else 1][:].rearrange("p (h q) -> p h q", h=4),
                                 ACT.Copy).then_inc(probsT_set, 1)
            for g in range(NG):
                act.wait_ge(pooled, g + 1)
                s.activation(mixT[:, 4 + g, :], bank[2 + g][:], ACT.Copy, scale=col(V_SCALE + g, 1)).then_inc(pooled_set, 1)

            for t in range(NT):
                act.wait_ge(h_set, t + 1)
                s.activation(normed[:, t, :], hx[:, t, :], ACT.Square, accum_out=sq[:, t:t + 1]).then_inc(squared, 1)
                act.wait_ge(var_set, 6 + t)
                s.activation(rstd[:, t:t + 1], rstd[:, t:t + 1], ACT.Sqrt).then_inc(rooted, 1)
            act.dma_start(sums[0:SEQ, :].rearrange("(t p) d -> p t d", p=P), hx[:]).then_inc(sums_set, 16)
            act.wait_ge(xn_set, 9)
            act.dma_start(normed_rows.rearrange("(t p) d -> p t d", p=P), normed[:, :, :]).then_inc(normed_stored, 16)
            act.wait_ge(top_set, 1)
            s.activation(top_e[:], top_e[:], ACT.Exp).then_inc(top_exp, 1)

            s.activation(sink_e[:], sink_e[:], ACT.Copy).then_inc(y_scaled, 1)

            act.wait_ge(rounds_set, 1)
            rounds = act.value_load(rounds_i[0:1, 0:1], min_val=1, max_val=ROUNDS)
            with act.Fori(0, rounds) as r:
                with act.Fori(0, BODIES) as b:
                    for j in range(UNROLL):
                        A = r * NE + b * UNROLL + j
                        for f in range(KC):
                            act.wait_ge(gate_capped, A * 8 + (f + 1))
                            s.activation(glu_t[:, f, :], gate_t[:, f, :], ACT.Sigmoid, scale=ALPHA).then_inc(sigmoids, 1)
                        for h in range(2):
                            act.wait_ge(y_T, A * 2 + (h + 1))
                            if h == 0:
                                act.wait_ge(sums_landed, A * 16 + FIRST_SUMS - 16)
                            s.activation(y_rows[j % 2][:, h * 512:(h + 1) * 512], bank[6 + h][0:CAP, :], ACT.Copy,
                                         scale=gate_c[0:CAP, j:j + 1]).then_inc(y_scaled, 1)

            for t in range(NT):
                act.wait_ge(final_in[t], 16)
                s.activation(normed[:, t, :], hx[:, t, :], ACT.Square, accum_out=sq[:, t:t + 1]).then_inc(squared, 1)
                act.wait_ge(var_set, 10 + t)
                s.activation(rstd[:, t:t + 1], rstd[:, t:t + 1], ACT.Sqrt).then_inc(rooted, 1)

        @block.vector
        def _(dve):
            v = nc.vector
            seq = [0]

            def then(ins):
                seq[0] += 1
                ins.then_inc(dve_seq, 1)
                dve.wait_ge(dve_seq, seq[0])

            def norm(t, done, src, dst, n=P):
                dve.wait_ge(squared, done + 1)
                v.tensor_scalar(rstd[0:n, t:t + 1], sq[0:n, t:t + 1], 1.0 / D, EPS, ALU.mult, ALU.add).then_inc(var_set, 1)
                dve.wait_ge(rooted, done + 1)
                then(v.reciprocal(rstd[0:n, t:t + 1], rstd[0:n, t:t + 1]))
                return v.tensor_scalar(dst, src, rstd[0:n, t:t + 1], None, ALU.mult).then_inc(xn_set, 1)

            v.memset(block_of[:], 0.0)
            then(v.memset(unseen[:], 0.0))
            for q in (0, 64):
                v.memset(block_of[q:q + 1, 0:64], 1.0)
                v.memset(block_of[q + 32:q + 33, 64:128], 1.0)
                v.memset(unseen[q:q + 1, :, PREV + 64:KEYS], NEG)
                v.memset(unseen[q + 32:q + 33, :, 0:64], NEG)
                v.memset(unseen[q:q + 1, 0, 0:64], NEG)
            dve.wait_ge(vecs_T, 1)
            v.tensor_copy(vec[:, 0:29], bank[7][:, 0:29]).then_inc(vecs_set, 1)
            dve.wait_ge(consts_set, 5)
            v.tensor_copy(bias[:, 0, 0:NE * KC], bank[5][:, 0:NE * KC])
            v.tensor_scalar(bias[:, 1, 0:NE * KC], bank[5][:, 256:256 + NE * KC], 1.0, None, ALU.add)
            v.tensor_copy(bias[:, 2, 0:NE * KC], bank[6][:, 0:NE * KC]).then_inc(vecs_set, 1)
            dve.wait_ge(vecs_set, 2)

            def u_out(t):
                for h in range(2):
                    dve.wait_ge(u_T, 2 * t + h + 1)
                    v.tensor_tensor(uT[:, 4 * h:4 * h + 4, t * P:(t + 1) * P],
                                    bank[(2 * t + h) % 4][:].rearrange("p (k n) -> p k n", k=4),
                                    spread(col(VG_MIX + 4 * h, 4), P), ALU.mult).then_inc(u_set, 1)

            for t in range(NT):
                norm(t, t, hx[:, t, :], xn[:, t, :])
                if t:
                    u_out(t - 1)
            norm(NT, NT, meta_x, meta_n, META)
            u_out(NT - 1)
            dve.wait_ge(u_T, 2 * NT + 1)
            v.tensor_tensor(uT_meta[:], bank[4][:, 0:KC * META].rearrange("p (k n) -> p k n", k=KC),
                            spread(col(VG_MIX, KC), META), ALU.mult).then_inc(u_set, 1)

            v.memset(k_prev[:, 0, 0:64], 0.0)
            v.memset(v_prev[0:64, 0, :], 0.0)
            dve.wait_ge(proj_set, 2)
            for m in range(1, NT):
                v.tensor_copy(k_prev[:, m, 0:64], kT[:, m * P - 64:m * P])
                v.tensor_copy(k_prev[:, m, 64:PREV], k_prev[:, 0, 64:PREV])
            dve.wait_ge(proj, 3)
            dve.wait_ge(consts_in, 16 * 5)
            then(v.tensor_tensor(v_own, bank[6][:].rearrange("p (m n) -> p m n", m=NT),
                                 bv[:].unsqueeze(1).to_broadcast([P, NT, P]), ALU.add))
            for m in range(NT):
                v.tensor_tensor(v_prev[64:PREV, m, :], bank[5][0:META, 128:256], bv[0:META, :], ALU.add)
                if m:
                    i = v.tensor_copy(v_prev[0:64, m, :], v_own[64:128, m - 1, :])
            i.then_inc(v_set, 1)

            def pool_windows(g):
                dve.wait_ge(p_set, g + 1)
                src, w, lo = pT[:, g, :], 1, 0
                for i in range(g + 1):
                    dst = wsum[i % 2]
                    then(v.tensor_tensor(dst[:, lo + w:L], src[:, lo + w:L], src[:, lo:L - w], ALU.add))
                    src, lo, w = dst, lo + w, 2 * w
                v.scalar_tensor_tensor(out=diffT[:, g, :], in0=src[:, META:L], scalar=1.0 / POOL_WINDOWS[g],
                                       in1=pT[:, g, META:L], op0=ALU.mult, op1=ALU.subtract).then_inc(diff_set, 1)

            for m in range(NT):
                dve.wait_ge(scored, m + 1)
                for i in range(4):
                    ins = v.tensor_reduce(mx[:, 2 * i:2 * i + 2],
                                          bank[i][:, 0:2 * KEYS].rearrange("p (h k) -> p h k", h=2), AX.X, ALU.max)
                then(ins)
                then(v.scalar_tensor_tensor(out=mx[:], in0=mx[:], scalar=SCALE, in1=sinks[:], op0=ALU.mult, op1=ALU.max))
                if m:
                    dve.wait_ge(exp_set, m)
                v.tensor_tensor(sink_e[:], sinks[:], mx[:], ALU.subtract)
                v.tensor_scalar(negm[:], mx[:], -1.0, None, ALU.mult).then_inc(max_set, 1)
                if m:
                    pool_windows(m - 1)
                dve.wait_ge(exp_set, m + 1)
                then(v.tensor_tensor(den[:], den[:], sink_e[:], ALU.add))
                then(v.reciprocal(den[:], den[:]))
                v.tensor_tensor(probs[:], probs[:], spread(den[:], KEYS), ALU.mult).then_inc(probs_set, 1)
                for g in range(2):
                    dve.wait_ge(probs_T, 2 * m + g + 1)
                    v.tensor_copy(probsT_prev, bank[5 if g == 0 else 0][0:PREV, :].rearrange("p (h q) -> p h q", h=4)
                                  ).then_inc(probsT_set, 1)
                dve.wait_ge(attended, m + 1)
                v.tensor_copy(mixT[:, 0:4, m * P:(m + 1) * P], bank[7][:].rearrange("p (c q) -> p c q", c=4)
                              ).then_inc(mix_set, 1)

            pool_windows(NG - 1)

            def residual(t):
                dve.wait_ge(mixed, t + 1)
                for h in range(2):
                    i = v.tensor_tensor(hx[:, t, h * 512:(h + 1) * 512], bank[2 * t + h][:],
                                        hx[:, t, h * 512:(h + 1) * 512], ALU.add)
                i.then_inc(h_set, 1)

            def f_out(t):
                for h in range(2):
                    dve.wait_ge(f_T, 2 * t + h + 1)
                    v.tensor_tensor(fT[:, 4 * h:4 * h + 4, t * P:(t + 1) * P],
                                    bank[2 * t + h][:].rearrange("p (k n) -> p k n", k=4),
                                    spread(col(VG_FFN + 4 * h, 4), P), ALU.mult).then_inc(f_set, 1)

            def top4(t):
                dve.wait_ge(routed, t + 1)
                then(v.tensor_tensor(logits[:, t, :], bank[2 * t][:, 0:NE], b_router[:], ALU.add))
                then(v.max(top[:, t, :], logits[:, t, :]))
                then(v.max_index(top_at[:, t, :], top[:, t, :], logits[:, t, :]))

            for t in range(NT):
                residual(t)
                norm(t, NT + 1 + t, hx[:, t, :], normed[:, t, :])
                if t:
                    f_out(t - 1)
                    top4(t - 1)
            f_out(NT - 1)
            top4(NT - 1)
            v.tensor_copy(top_f[:], top_at[:])
            v.tensor_tensor(top_e[:], top[:, :, 0:TOPK], top[:, :, 0:1].to_broadcast([P, NT, TOPK]),
                            ALU.subtract).then_inc(top_set, 1)
            dve.wait_ge(top_exp, 1)
            then(v.tensor_reduce(top_s[:], top_e[:], AX.X, ALU.add))
            then(v.reciprocal(top_s[:], top_s[:]))
            then(v.tensor_tensor(top_e[:], top_e[:], spread(top_s[:], TOPK), ALU.mult))
            for t in range(NT):
                then(v.tensor_tensor(chosen[:], iota_exp[:].unsqueeze(1).to_broadcast([P, TOPK, NE]),
                                     spread(top_f[:, t, 0:TOPK], NE), ALU.is_equal))
                v.tensor_reduce(mask[:, t, :], chosen[:].rearrange("p k e -> p e k"), AX.X, ALU.add)
                then(v.tensor_tensor(chosen_g[:], chosen[:], spread(top_e[:, t, :], NE), ALU.mult))
                then(v.tensor_reduce(gates[:, t, 0:NE], chosen_g[:].rearrange("p k e -> p e k"), AX.X, ALU.add))
            v.tensor_copy(mask_b[:], mask[:]).then_inc(mask_set, 1)
            dve.wait_ge(mask_set, 1)
            then(v.tensor_scalar(mask[:], mask[:], FAR, CAP - FAR, ALU.mult, ALU.add))
            dve.wait_ge(ranked, 1)
            v.tensor_tensor(ranks[:, :, 0:NE], bank[2][:, 0:NT * NE].rearrange("p (t e) -> p t e", t=NT),
                            mask[:], ALU.add)
            then(v.tensor_reduce(count[:], bank[3][:, 0:NE], AX.X, ALU.max))
            then(v.tensor_scalar(over[:], steps[:], count[:], None, ALU.is_lt))
            then(v.tensor_reduce(rounds_f[:], over[:], AX.X, ALU.add))
            v.tensor_copy(rounds_i[:], rounds_f[:]).then_inc(rounds_set, 1)
            dve.wait_ge(rounds_set, 1)
            rounds = dve.value_load(rounds_i[0:1, 0:1], min_val=1, max_val=ROUNDS)

            def mark(e):
                v.tensor_tensor(hot, iota_cap[:].unsqueeze(1).to_broadcast([P, NT, CAP]),
                                ranks[:, :, bass.ds(e, 1)].to_broadcast([P, NT, CAP]), ALU.is_equal)
                v.tensor_copy(place_in[:, :, 1:2], gates[:, :, bass.ds(e, 1)]).then_inc(hot_set, 1)

            def places(j, I):
                dve.wait_ge(place_ready, I + 1)
                j = j % UNROLL
                src = bank[5][0:CAP, 4 * CAP:4 * CAP + 3]
                v.tensor_copy(from_row[0:CAP, j:j + 1], src[:, 0:1])
                v.tensor_copy(gate_c[0:CAP, j:j + 1], src[:, 1:2])
                v.tensor_scalar(to_f[0:CAP], src[:, 2:3], spare[0:CAP, 1:2], spare[0:CAP, 0:1],
                                ALU.mult, ALU.add).then_inc(ranks_moved, 1)
                return src

            def places_end(j, src, n):
                dve.wait_ge(ranks_moved, n)
                j = j % UNROLL
                v.tensor_tensor(to_row[0:CAP, j:j + 1], to_f[0:CAP], src[:, 0:1], ALU.add).then_inc(place_set, 1)

            def x_out(j, n):
                for h in range(2):
                    dve.wait_ge(x_T, n + h + 1)
                    v.tensor_tensor(xT[j % 2][:, 4 * h:4 * h + 4, :],
                                    bank[6 + h][:, 0:4 * CAP].rearrange("p (k n) -> p k n", k=4),
                                    spread(col(VG_FFN + 4 * h, 4), CAP), ALU.mult).then_inc(xT_set, 1)

            with dve.Fori(0, rounds) as r:
                v.tensor_scalar(ranks[:], ranks[:], -float(CAP), None, ALU.add).then_inc(ranks_moved, 1)
                dve.wait_ge(ranks_moved, r * (NEP + 1) + 1)
                dve.wait_ge(sums_landed, r * (16 * NE) + FIRST_SUMS)
                for j in range(AHEAD):
                    mark(j)
                    src = places(j, r * NEP + j)
                    places_end(j, src, r * (NEP + 1) + (2 + j))
                x_out(0, r * (2 * (NE + 1)))
                with dve.Fori(0, BODIES) as b:
                    for j in range(UNROLL):
                        A = r * NE + b * UNROLL + j
                        dve.wait_ge(bias_set, r * (NE + 1) + b * UNROLL + (j + 1))
                        be = bias_e[:, j % 2]
                        for half in range(2):
                            for f in range(4 * half, 4 * half + 4):
                                dve.wait_ge(gate_ready, A * 8 + (f + 1))
                                v.tensor_scalar(gate_t[:, f, :], bank[f % 4][:, 0:CAP],
                                                be[:, 0, f:f + 1], LIMIT, ALU.add, ALU.min).then_inc(gate_capped, 1)
                            for f in range(4 * half, 4 * half + 4):
                                dve.wait_ge(sigmoids, A * 8 + (f + 1))
                                v.tensor_tensor(glu_t[:, f, :], gate_t[:, f, :], glu_t[:, f, :], ALU.mult
                                                ).then_inc(glu_set, 1)
                                dve.wait_ge(up_ready, A * 8 + (f + 1))
                                v.tensor_scalar(up_t[:, f, :], bank[f % 4][:, 0:CAP],
                                                be[:, 1, f:f + 1], LIMIT + 1.0, ALU.add, ALU.min).then_inc(up_capped, 1)
                                dve.wait_ge(up_capped, A * 8 + (f + 1))
                                v.scalar_tensor_tensor(out=act_t[:, f, :], in0=up_t[:, f, :], scalar=1.0 - LIMIT,
                                                       in1=glu_t[:, f, :], op0=ALU.max, op1=ALU.mult
                                                       ).then_inc(act_set, 1)
                            if half == 0:
                                mark(b * UNROLL + (j + AHEAD))
                        dve.wait_ge(sums_landed, A * 16 + FIRST_SUMS - 16)
                        src = places(j + AHEAD, r * NEP + b * UNROLL + (j + AHEAD))
                        x_out(j + 1, (r * (NE + 1) + b * UNROLL + (j + 1)) * 2)
                        places_end(j + AHEAD, src, r * (NEP + 1) + b * UNROLL + (j + AHEAD + 2))
                        for h in range(2):
                            dve.wait_ge(down_ready, A * 2 + (h + 1))
                            v.tensor_tensor(yT[:, 4 * h:4 * h + 4, :],
                                            bank[4 + h][:, 0:4 * CAP].rearrange("p (k n) -> p k n", k=4),
                                            spread(be[:, 2, 4 * h:4 * h + 4], CAP), ALU.add).then_inc(y_biased, 1)

            for t in range(NT):
                dve.wait_ge(final_in[t], 16)
                norm(t, 2 * NT + 1 + t, hx[:, t, :], hx[:, t, :])
                dve.wait_ge(xn_set, 10 + t)
                dve.wait_ge(g_final_in, 16)
                v.tensor_tensor(normed[:, t, :], hx[:, t, :], g_final, ALU.mult).then_inc(out_set, 1)

        @block.tensor
        def _(pe):
            mm = nc.tensor.matmul

            def tr(dst, src):
                return mm(dst, src, ident[0:src.shape[0], 0:src.shape[0]], start=True, stop=True, is_transpose=True)

            pe.wait_ge(consts_set, 2)
            pe.wait_ge(vec_in, 16 * 11)
            for i in range(3):
                for h in range(2):
                    c = (2 * i + h) * P
                    tr(bank[5 + c // 512][:, c % 512:c % 512 + P], bias_rows[:, i, h, :])
            tr(bank[7][:, 0:29], vec_rows[0:29, :]).then_inc(vecs_T, 1)
            for t in range(NT):
                pe.wait_ge(xn_set, t + 1)
                if t >= 2:
                    pe.wait_ge(u_set, 2 * (t - 1))
                for h in range(2):
                    for k in range(4):
                        i = tr(bank[(2 * t + h) % 4][:, k * P:(k + 1) * P], xn[:, t, (4 * h + k) * P:(4 * h + k + 1) * P])
                    i.then_inc(u_T, 1)
            pe.wait_ge(xn_set, NT + 1)
            for k in range(KC):
                i = tr(bank[4][:, k * META:(k + 1) * META], meta_n[:, k * P:(k + 1) * P])
            i.then_inc(u_T, 1)
            pe.wait_ge(u_set, 2 * NT + 1)
            pe.wait_ge(vecs_set, 2)

            def project(dst, lhs, rhs):
                for k in range(KC):
                    i = mm(dst, lhs(k), rhs(k), start=k == 0, stop=k == KC - 1)
                return i

            pe.wait_ge(wkv_in, 16)
            project(bank[0][:, 0:SEQ], lambda k: wkv[:, k, 0:128], lambda k: uT[:, k, :]).then_inc(proj, 1)
            pe.wait_ge(wp_in, 16)
            project(bank[5][:, 0:META], lambda k: wkv[:, k, 0:128], lambda k: uT_meta[:, k, :])
            for c in range(NG):
                project(bank[5][:, META * (1 + c):META * (2 + c)], lambda k: wp[:, k, c * P:(c + 1) * P],
                        lambda k: uT_meta[:, k, :])
            project(bank[5][0:META, 128:256], lambda k: uT_meta[:, k, :], lambda k: wkv[:, k, 128:256]).then_inc(proj, 1)
            for m in range(NT):
                i = project(bank[6][:, m * P:(m + 1) * P], lambda k: uT[:, k, m * P:(m + 1) * P],
                            lambda k: wkv[:, k, 128:256])
            i.then_inc(proj, 1)
            pe.wait_ge(wq_in, 16)
            for c in range(4):
                project(bank[1 + c][:], lambda k: wq[:, k, c * P:(c + 1) * P], lambda k: uT[:, k, :]).then_inc(proj, 1)

            pe.wait_ge(proj_set, 6)
            pe.wait_ge(v_set, 1)
            for m in range(NT):
                if m:
                    pe.wait_ge(probsT_set, 4 * m)
                for h in range(HEADS):
                    g, c = divmod(h, HALF)
                    rows = slice(64 * g, 64 * g + 64)
                    dst = bank[h // 2][:, (h % 2) * KEYS:(h % 2 + 1) * KEYS]
                    q = qT[rows, c, m * P:(m + 1) * P]
                    mm(dst, block_of[rows, :], unseen[rows, min(m, 1), :], start=True, stop=False)
                    mm(dst[:, 0:PREV], q, k_prev[rows, m, :], start=False, stop=False)
                    i = mm(dst[:, PREV:KEYS], q, kT[rows, m * P:(m + 1) * P], start=False, stop=True)
                i.then_inc(scored, 1)
                if m:
                    pe.wait_ge(p_set, m)
                project(bank[4][:], lambda k: wp[:, k, m * P:(m + 1) * P], lambda k: uT[:, k, :]).then_inc(proj, 1)
                pe.wait_ge(probs_set, m + 1)
                for g in range(2):
                    prev, own = (bank[5], bank[6]) if g == 0 else (bank[0], bank[1])
                    for c in range(HALF):
                        tr(prev[0:PREV, c * P:(c + 1) * P], probs[:, HALF * g + c, 0:PREV])
                        i = tr(own[:, c * P:(c + 1) * P], probs[:, HALF * g + c, PREV:KEYS])
                    i.then_inc(probs_T, 1)
                    pe.wait_ge(probsT_set, 4 * m + 2 * g + 2)
                    if g == 0 and m:
                        pe.wait_ge(mix_set, m)
                    for c in range(HALF):
                        dst = bank[7][64 * g:64 * g + 64, c * P:(c + 1) * P]
                        mm(dst, v_prev[0:PREV, m, 64 * g:64 * g + 64], probsT_prev[:, c, :], start=True, stop=False)
                        i = mm(dst, v_own[:, m, 64 * g:64 * g + 64], probsT_own[:, c, :], start=False, stop=True)
                i.then_inc(attended, 1)

            for g in range(NG):
                pe.wait_ge(diff_set, g + 1)
                mm(bank[2 + g][:], w_pool[:, g, :], diffT[:, g, :], start=True, stop=True).then_inc(pooled, 1)

            pe.wait_ge(wout_in, 16 * 2)
            pe.wait_ge(mix_set, NT)

            def logits_of(t):
                pe.wait_ge(xn_set, NT + 2 + t)
                for h in range(2):
                    for k in range(4):
                        i = tr(bank[2 * t + h][:, k * P:(k + 1) * P],
                               normed[:, t, (4 * h + k) * P:(4 * h + k + 1) * P])
                    i.then_inc(f_T, 1)

            def route(t):
                pe.wait_ge(f_set, 2 * t + 2)
                project(bank[2 * t][:, 0:NE], lambda k: fT[:, k, t * P:(t + 1) * P],
                        lambda k: w_router[:, k, :]).then_inc(routed, 1)

            pe.wait_ge(pooled_set, NG)
            for t in range(NT):
                for h in range(2):
                    i = project(bank[2 * t + h][:], lambda k: mixT[:, k, t * P:(t + 1) * P], lambda k: wout[h][:, k, :])
                i.then_inc(mixed, 1)
                if t >= 1:
                    logits_of(t - 1)
                if t >= 2:
                    route(t - 2)
            logits_of(NT - 1)
            route(NT - 2)
            route(NT - 1)

            pe.wait_ge(mask_set, 1)
            for t in range(NT):
                dst = bank[2][:, t * NE:(t + 1) * NE]
                for q in range(t):
                    mm(dst, ones[:], mask_b[:, q, :], start=q == 0, stop=False)
                mm(dst, earlier[:], mask_b[:, t, :], start=t == 0, stop=True)
            for q in range(NT):
                i = mm(bank[3][:, 0:NE], ones[:], mask_b[:, q, :], start=q == 0, stop=q == NT - 1)
            i.then_inc(ranked, 1)

            pe.wait_ge(rounds_set, 1)
            rounds = pe.value_load(rounds_i[0:1, 0:1], min_val=1, max_val=ROUNDS)

            def find(I):
                pe.wait_ge(hot_set, I + 1)
                for t in range(NT):
                    i = mm(bank[5][0:CAP, 4 * CAP:4 * CAP + 3], hot[:, t, :], place_in[:, t, :],
                           start=t == 0, stop=t == NT - 1)
                i.then_inc(place_ready, 1)

            def x_transpose(j, G, A):
                pe.wait_ge(gathered[j % 2], G * 16 + 16)
                pe.wait_ge(y_scaled, A * 2 + 1)
                for h in range(2):
                    for k in range(4):
                        i = tr(bank[6 + h][:, k * CAP:(k + 1) * CAP], x_rows[j % 2][:, (4 * h + k) * P:(4 * h + k + 1) * P])
                    i.then_inc(x_T, 1)

            per_round = NEP // 2
            with pe.Fori(0, rounds) as r:
                find(r * NEP)
                find(r * NEP + 1)
                x_transpose(0, r * per_round, r * NE)
                with pe.Fori(0, BODIES) as b:
                    for j in range(UNROLL):
                        A = r * NE + b * UNROLL + j
                        X = r * (NE + 1) + b * UNROLL + j
                        pe.wait_ge(xT_set, X * 2 + 2)
                        for u in range(4):
                            w = slot_of(j, u)
                            pe.wait_ge(weights_in[w], (r * 24 + b * 3 + ((UNITS * j + u) // SLOTS + 1)) * 16)
                            half, kind = divmod(u, 2)
                            for f in range(4):
                                if kind:
                                    pe.wait_ge(gate_capped, A * 8 + (4 * half + f + 1))
                                elif half:
                                    pe.wait_ge(up_capped, A * 8 + (f + 1))
                                i = project(bank[f][:, 0:CAP],
                                            lambda k: slot[w][:, k, f * P:(f + 1) * P], lambda k: xT[j % 2][:, k, :])
                                i.then_inc(up_ready if kind else gate_ready, 1)
                        find(r * NEP + b * UNROLL + (j + AHEAD))
                        x_transpose(j + 1, r * per_round + b * 2 + (j + 1) // 2, A)
                        for h in range(2):
                            w = slot_of(j, 4 + h)
                            pe.wait_ge(weights_in[w], (r * 24 + b * 3 + ((UNITS * j + 4 + h) // SLOTS + 1)) * 16)
                            if h == 1:
                                pe.wait_ge(place_set, r * NEP + b * UNROLL + (j + AHEAD + 1))
                            for d in range(4):
                                for f in range(KC):
                                    if h == 0 and d == 0:
                                        pe.wait_ge(act_set, A * 8 + (f + 1))
                                    i = mm(bank[4 + h][:, d * CAP:(d + 1) * CAP], slot[w][:, f, d * P:(d + 1) * P],
                                           act_t[:, f, :], start=f == 0, stop=f == KC - 1)
                            i.then_inc(down_ready, 1)
                        pe.wait_ge(xT_set, X * 2 + 4)
                        for h in range(2):
                            pe.wait_ge(y_biased, A * 2 + (h + 1))
                            for k in range(4):
                                i = tr(bank[6 + h][0:CAP, k * P:(k + 1) * P], yT[:, 4 * h + k, :])
                            i.then_inc(y_T, 1)
                pe.wait_ge(gathered[1], (r * per_round + per_round) * 16)


_SHAPE = (1, SEQ, D)


def kernel(**inputs):
    import numpy as _np
    import concourse.bacc as _bacc
    from concourse import mybir as _mybir
    from concourse.bass_utils import run_bass_kernel_spmd as _run

    nc = _bacc.Bacc("TRN2", target_bir_lowering=False, num_devices=1)
    def pairs(x, axis):
        at = [2 * h + g for g in range(2) for h in range(HALF)]
        order = _np.argsort(at)
        parts = _np.split(_np.asarray(x), [HEADS * HD], axis=axis)
        heads = _np.split(parts[0], HEADS, axis=axis)
        return _np.concatenate([heads[i] for i in order] + [parts[1]], axis=axis)

    inputs = dict(inputs, w_in=pairs(inputs["w_in"], 2), b_in=pairs(inputs["b_in"], 1),
                  w_out=pairs(inputs["w_out"], 1))
    arrays, args = {}, {}
    for name, x in inputs.items():
        x = _np.ascontiguousarray(x)
        arrays[f"in_{name}"] = x
        args[name] = nc.dram_tensor(f"in_{name}", x.shape, _mybir.dt.from_np(x.dtype), kind="ExternalInput").ap()
    out = nc.dram_tensor("out_0", _SHAPE, _mybir.dt.float32, kind="ExternalOutput").ap()
    build(nc, args, out)
    r = _run(nc, [arrays], core_ids=[0])
    return r.results[0]["out_0"]
```

```python
from contextlib import ExitStack

import concourse.bass as bass
from concourse import mybir

F32 = mybir.dt.float32
BF16 = mybir.dt.bfloat16
F32R = mybir.dt.float32r
U32 = mybir.dt.uint32
I32 = mybir.dt.int32
ALU = mybir.AluOpType
ACT = mybir.ActivationFunctionType
AX = mybir.AxisListType

P = 128
D = 1024
KC = D // P
SEQ = 512
NT = SEQ // P
META = 16
HD = 64
SCALE = HD ** -0.5
HEADS = 8
HALF = HEADS // 2
PREV = 64 + META
KEYS = PREV + P
NG = 4
POOL_WINDOWS = (2, 4, 8, 16)
NE = 32
TOPK = 4
CAP = 96
ROUNDS = -(-SEQ // CAP)
LIMIT, ALPHA = 7.0, 1.702
EPS = 1e-5
NEG = -1e30
FAR = 1.0e6
UNROLL = 4
BODIES = NE // UNROLL
UNITS = 6
COLS = 512
AHEAD = 2
NEP = NE + AHEAD
FIRST_SUMS = 32


def build(nc, a, out):
    ctx = ExitStack()
    with ctx:
        def sb(name, shape, dt=F32):
            return ctx.enter_context(nc.sbuf_tensor(name, shape, dt))

        def lent(name, shape):
            with nc.sbuf_tensor(name, shape, F32) as t:
                return t

        def sem(name):
            return ctx.enter_context(nc.semaphore(name))

        normed_rows = nc.dram_tensor("normed_rows", (SEQ, D), F32).ap()
        sums = nc.dram_tensor("sums", (SEQ + CAP, D), F32).ap()

        ring = []
        ring_low = []
        for u in range(UNITS):
            if u < 4:
                ring.append(lent(f"ring{u}", [P, KC * COLS]))
                ring_low.append(sb(f"ring_low{u}", [P, KC * COLS], F32R))
            else:
                ring.append(sb(f"ring{u}", [P, KC * COLS]))
        wout_rows, high_of = [], []
        for h in range(2):
            wout_rows.append(lent(f"wout{h}", [P, KC * COLS]))
            high_of.append(sb(f"high_of_{('gate', 'up')[h]}", [P, KC * COLS], F32R))
        slot = [r[:].rearrange("p (k n) -> p k n", k=KC) for r in ring]
        uT = ring[0][:].rearrange("p (k n) -> p k n", k=KC)
        qT = ring[1][:, 0:4 * SEQ].rearrange("p (c n) -> p c n", c=4)
        diffT = ring[1][:, 4 * SEQ:8 * SEQ].rearrange("p (c n) -> p c n", c=4)
        probs = ring[2][:, 0:HEADS * KEYS].rearrange("p (h k) -> p h k", h=HEADS)
        o = HEADS * KEYS
        probsT_prev = ring[2][0:PREV, o:o + 512].rearrange("p (h q) -> p h q", h=4)
        probsT_own = ring[2][:, o + 512:o + 1024].rearrange("p (h q) -> p h q", h=4)
        o += 1024
        L = META + SEQ
        wsum = [ring[2][:, o + i * L:o + (i + 1) * L] for i in range(2)]
        wq, wp = slot[3], slot[4]
        wkv = ring[5][:, 0:KC * 256].rearrange("p (k n) -> p k n", k=KC)
        o = KC * 256
        kT = ring[5][:, o:o + SEQ]
        o += SEQ
        k_prev = ring[5][:, o:o + NT * PREV].rearrange("p (m k) -> p m k", m=NT)
        o += NT * PREV
        v_own = ring[5][:, o:o + NT * P].rearrange("p (m n) -> p m n", m=NT)
        o += NT * P
        v_prev = ring[5][:, o:o + NT * P].rearrange("p (m n) -> p m n", m=NT)
        wout = [h[:].rearrange("p (k n) -> p k n", k=KC) for h in wout_rows]

        hx = sb("hx", [P, NT, D])
        work = sb("work", [P, 2 * KC * SEQ])
        work_2 = lent("work_2", [P, KC * SEQ])
        x_split = sb("x_split", [P, 2 * KC * CAP], F32R)
        y_both = sb("y_both", [CAP, 2 * D])
        gate_parts = sb("gate_parts", [P, NT, 3 * NEP], BF16)
        hot = sb("hot", [P, NT, CAP], BF16)
        left = KC * SEQ - 2 * KC * CAP - 2 * D - NT * (3 * NEP + CAP) // 2
        assert left >= 0
        sb("work_2_end", [P, left])
        third = [work[:, 0:KC * SEQ], work[:, KC * SEQ:2 * KC * SEQ], work_2[:]]
        xn = third[0].rearrange("p (t d) -> p t d", t=NT)
        mixT = third[0].rearrange("p (k n) -> p k n", k=KC)
        normed = third[1].rearrange("p (t d) -> p t d", t=NT)
        pT = third[1][:, 0:NG * L].rearrange("p (g n) -> p g n", g=NG)
        meta_x = third[1][0:META, NG * L:NG * L + D]
        vec_rows = third[1][0:32, NG * L + D:NG * L + D + P]
        bias_raw = third[2][0:3 * NE, 0:3 * D]
        meta_n = third[2][0:META, 3 * D:4 * D]
        fT = third[2].rearrange("p (k n) -> p k n", k=KC)
        o = 0

        def carve(n):
            nonlocal o
            o += n
            return work[:, o - n:o]

        x_rows = [carve(D)[0:CAP] for _ in range(2)]
        x_f = carve(KC * CAP).rearrange("p (k n) -> p k n", k=KC)
        x_high, x_low = (x_split[:, i * KC * CAP:(i + 1) * KC * CAP].rearrange("p (k n) -> p k n", k=KC)
                         for i in range(2))
        gate_t = carve(D)[0:CAP]
        glu_t = carve(D)[0:CAP]
        up_t = carve(D)[0:CAP]
        act_t = up_t
        actT = carve(KC * CAP).rearrange("p (k n) -> p k n", k=KC)
        y_rows = [y_both[:, i * D:(i + 1) * D] for i in range(2)]
        g_final = ring[2][:, 0:D]

        ident = sb("ident", [P, P])
        iota_cap = sb("iota_cap", [P, CAP])
        iota_exp = sb("iota_exp", [P, NE])
        steps = sb("steps", [P, ROUNDS])
        earlier = sb("earlier", [P, P], BF16)
        ones = sb("ones", [P, P], BF16)
        block_of = sb("block_of", [P, P], BF16)
        unseen = sb("unseen", [P, 2, KEYS], BF16)
        pace = sb("pace", [1, 2 * UNROLL + 1])
        zeros = sb("zeros", [CAP, D // 4])
        spare = sb("spare", [P, 2])
        place_in = sb("place_in", [P, NT, 6], BF16)
        vec = sb("vec", [P, 32])
        VG_MIX, VG_FFN, VB_Q, VB_K, VB_P, V_SCALE = 0, 8, 16, 20, 21, 25
        bv = ring[2][:, 4096 - P:4096]
        sinks = sb("sinks", [P, HEADS])
        b_router = sb("b_router", [P, NE])
        w_router = sb("w_router", [P, KC, NE])
        o = NG * L + D + P
        w_pool = third[1][:, o:o + NG * P].rearrange("p (g n) -> p g n", g=NG)
        o += NG * P
        uT_meta = third[1][:, o:o + KC * META].rearrange("p (k n) -> p k n", k=KC)
        sq = sb("sq", [P, 5])
        rstd = sb("rstd", [P, 5])
        mx = sb("mx", [P, HEADS])
        negm = sb("negm", [P, HEADS])
        sink_e = sb("sink_e", [P, HEADS])
        den = sb("den", [P, HEADS])
        logits = sb("logits", [P, NT, NE])
        top = sb("top", [P, NT, 8])
        top_at = sb("top_at", [P, NT, 8], U32)
        top_f = sb("top_f", [P, NT, 8])
        top_e = sb("top_e", [P, NT, TOPK])
        top_s = sb("top_s", [P, NT])
        chosen = sb("chosen", [P, TOPK, NE])
        chosen_g = sb("chosen_g", [P, TOPK, NE])
        mask = sb("mask", [P, NT, NE])
        mask_b = sb("mask_b", [P, NT, NE], BF16)
        ranks = sb("ranks", [P, NT, NEP])
        gates = logits
        count = sb("count", [P, 1])
        over = sb("over", [P, ROUNDS])
        rounds_f = sb("rounds_f", [P, 1])
        rounds_i = sb("rounds_i", [P, 1], I32)
        bias_parts = sb("bias_parts", [3 * NE, 3 * D], BF16)
        part_of = sb("part_of", [3 * NE, NE + 1], BF16)
        bias_row = sb("bias_row", [3 * NE, 2, CAP], BF16)
        minus_from = sb("minus_from", [3 * NE, 2])
        from_row = sb("from_row", [P, UNROLL], U32)
        to_row = sb("to_row", [P, UNROLL], U32)
        to_f = sb("to_f", [P, 1])
        token_f = sb("token_f", [P, 1])
        gate_c = sb("gate_c", [P, UNROLL])

        bank = [ctx.enter_context(nc.psum_tensor(f"bank{i}", [P, 512], F32)) for i in range(8)]

        x_in = [sem(f"x_in{t}") for t in range(NT)]
        meta_in, vec_in, consts_in = sem("meta_in"), sem("vec_in"), sem("consts_in")
        wkv_in, wq_in, wp_in, wout_in = sem("wkv_in"), sem("wq_in"), sem("wp_in"), sem("wout_in")
        weights_in = [sem(f"weights_in{i}") for i in range(UNITS)]
        consts_set = sem("consts_set")
        squared, rooted, var_set, xn_set = sem("squared"), sem("rooted"), sem("var_set"), sem("xn_set")
        vecs_T, vecs_set = sem("vecs_T"), sem("vecs_set")
        u_T, u_set = sem("u_T"), sem("u_set")
        proj, proj_set = sem("proj"), sem("proj_set")
        v_set = sem("v_set")
        scored, max_set, exp_set, probs_set = sem("scored"), sem("max_set"), sem("exp_set"), sem("probs_set")
        probs_T, probsT_set = sem("probs_T"), sem("probsT_set")
        attended, mix_set = sem("attended"), sem("mix_set")
        diff_set, pooled, pooled_set = sem("diff_set"), sem("pooled"), sem("pooled_set")
        p_set = sem("p_set")
        mixed, h_set, f_T, f_set, routed, logits_set = (
            sem("mixed"), sem("h_set"), sem("f_T"), sem("f_set"), sem("routed"), sem("logits_set"))
        top_set, top_exp = sem("top_set"), sem("top_exp")
        mask_set, ranked, rounds_set = sem("mask_set"), sem("ranked"), sem("rounds_set")
        normed_stored = sem("normed_stored")
        sums_set = sem("sums_set")
        g_final_in = sem("g_final_in")
        dve_seq = sem("dve_seq")
        ranks_moved, hot_set, place_ready, place_set = (
            sem("ranks_moved"), sem("hot_set"), sem("place_ready"), sem("place_set"))
        gathered = [sem(f"gathered{i}") for i in range(2)]
        x_T, xf_set, xh_set, xT_set, bias_set = (
            sem("x_T"), sem("xf_set"), sem("xh_set"), sem("xT_set"), sem("bias_set"))
        high_set, low_set, high_used = sem("high_set"), sem("low_set"), sem("high_used")
        gate_ready, gate_capped, sigmoids = sem("gate_ready"), sem("gate_capped"), sem("sigmoids")
        up_ready, up_capped, glu_set, act_set = sem("up_ready"), sem("up_capped"), sem("glu_set"), sem("act_set")
        act_T, actT_set = sem("act_T"), sem("actT_set")
        down_ready, y_scaled = sem("down_ready"), sem("y_scaled")
        bias_in, bias_step, parts_set = sem("bias_in"), sem("bias_step"), sem("parts_set")
        sums_landed = sem("sums_landed")
        final_in = [sem(f"final_in{t}") for t in range(NT)]
        out_set, stored = sem("out_set"), sem("stored")

        def col(v, n):
            return vec[:, v:v + n]

        def spread(ap, n):
            return ap.unsqueeze(2).to_broadcast([ap.shape[0], ap.shape[1], n])

        weight = [a["w_gate"], a["w_up"], a["w_gate"], a["w_up"], a["w_down"], a["w_down"]]
        which_half = [0, 0, 1, 1, 0, 1]

        def unit_src(at, u):
            c = which_half[u] * COLS
            whole = weight[u][0].rearrange("e d n -> (e d n)")
            return whole[bass.ds(at, D * D)].rearrange("(k p n) -> p k n", p=P, n=D)[:, :, c:c + COLS]

        def half_unit(ap, p):
            return ap[:, p * (KC // 2) * COLS:(p + 1) * (KC // 2) * COLS]

        block = ctx.enter_context(nc.Block())

        @block.sync
        def _(sp):
            xr = a["x"][0].rearrange("(t p) d -> p t d", p=P)
            for t in range(NT):
                sp.dma_start(hx[:, t, :], xr[:, t, :]).then_inc(x_in[t], 16)
            sp.dma_start(meta_x, a["meta_tokens"]).then_inc(meta_in, 16)
            w_in = a["w_in"][0].rearrange("(k p) n -> p k n", p=P)
            sp.dma_start(wkv, w_in[:, :, 512:768]).then_inc(wkv_in, 16)
            sp.dma_start(wq, w_in[:, :, 0:512]).then_inc(wq_in, 16)
            sp.dma_start(wp, w_in[:, :, 768:1280]).then_inc(wp_in, 16)
            w_out = a["w_out"][0].rearrange("(k p) n -> p k n", p=P)
            for h in range(2):
                sp.dma_start(wout[h], w_out[:, :, h * COLS:(h + 1) * COLS]).then_inc(wout_in, 16)

            start = sp.alloc_register("unit_start")

            def load(e, u, wait=None):
                if wait is not None:
                    sp.reg_mul(start, e, D * D)
                    sp.reg_sub(start, start, COLS)
                    at = sp.snap(start, min_val=D * D - COLS, max_val=(NE - 1) * D * D - COLS) + COLS
                    freed(u, wait)
                else:
                    at = e * D * D
                sp.dma_start(slot[u], unit_src(at, u)).then_inc(weights_in[u], 16)

            def freed(u, A):
                if u >= 4:
                    sp.wait_ge(down_ready, A * 2 + (u - 3))
                else:
                    sp.wait_ge(gate_ready if u % 2 == 0 else up_ready, A * 2 + (1 + u // 2))

            sp.wait_ge(proj, 7 + NG)
            for u in (0, 3, 4):
                load(0, u)
            sp.wait_ge(pooled, NG)
            for u in (1, 2, 5):
                load(0, u)

            sp.wait_ge(rounds_set, 1)
            rounds = sp.value_load(rounds_i[0:1, 0:1], min_val=1, max_val=ROUNDS)
            with sp.Fori(0, rounds) as r:
                with sp.Fori(0, NE - 1) as e:
                    for u in range(UNITS):
                        load(e + 1, u, r * NE + e)
                for u in range(2):
                    freed(u, r * NE + (NE - 1))
                    load(0, u)
                with sp.If(r + 1 < rounds):
                    for u in range(2, UNITS):
                        freed(u, r * NE + (NE - 1))
                        load(0, u)

            sp.wait_ge(up_ready, rounds * (2 * NE))
            sp.dma_start(g_final, a["norm_final_g"].partition_broadcast(P)).then_inc(g_final_in, 16)
            sp.wait_ge(sums_landed, rounds * (16 * NE) + FIRST_SUMS)
            sr = sums[0:SEQ, :].rearrange("(t p) d -> p t d", p=P)
            for t in range(NT):
                sp.dma_start(hx[:, t, :], sr[:, t, :]).then_inc(final_in[t], 16)
            outr = out[0].rearrange("(t p) d -> p t d", p=P)
            for t in range(NT):
                sp.wait_ge(out_set, t + 1)
                sp.dma_start(outr[:, t, :], normed[:, t, :]).then_inc(stored, 16)
            sp.wait_ge(stored, 16 * NT)

        @block.gpsimd
        def _(pool):
            g = nc.gpsimd
            g.memset(ident[:], 0.0).then_inc(consts_set, 1)
            pool.wait_ge(consts_set, 1)
            g.affine_select(out=ident[:], in_=ident[:], compare_op=ALU.not_equal, fill=1.0, base=0,
                            pattern=[[-1, P]], channel_multiplier=1).then_inc(consts_set, 1)
            g.memset(earlier[:], 1.0).then_inc(consts_set, 1)
            pool.wait_ge(consts_set, 3)
            g.affine_select(out=earlier[:], in_=earlier[:], compare_op=ALU.is_gt, fill=0.0, base=0,
                            pattern=[[1, P]], channel_multiplier=-1)
            g.memset(ones[:], 1.0)
            g.memset(zeros[:], 0.0)
            g.iota(iota_cap[:], pattern=[[1, CAP]], base=0, channel_multiplier=0, allow_small_or_imprecise_dtypes=True)
            g.iota(iota_exp[:], pattern=[[1, NE]], base=0, channel_multiplier=0, allow_small_or_imprecise_dtypes=True)
            g.iota(steps[:], pattern=[[CAP, ROUNDS]], base=0, channel_multiplier=0, allow_small_or_imprecise_dtypes=True)
            g.iota(spare[:, 0:1], pattern=[[1, 1]], base=SEQ, channel_multiplier=1, allow_small_or_imprecise_dtypes=True)
            g.iota(spare[:, 1:2], pattern=[[1, 1]], base=-SEQ, channel_multiplier=-1, allow_small_or_imprecise_dtypes=True)
            g.memset(place_in[:], 1.0).then_inc(consts_set, 1)
            pool.wait_ge(consts_set, 4)
            g.iota(place_in[:, :, 0:1], pattern=[[0, NT], [0, 1]], base=0, channel_multiplier=1,
                   allow_small_or_imprecise_dtypes=True)
            g.iota(place_in[:, :, 1:2], pattern=[[P, NT], [0, 1]], base=0, channel_multiplier=0,
                   allow_small_or_imprecise_dtypes=True)
            g.memset(ranks[:], -FAR)
            g.memset(part_of[:], 0.0)
            g.iota(minus_from[:], pattern=[[NE, 2]], base=-2 * NE, channel_multiplier=1,
                   allow_small_or_imprecise_dtypes=True).then_inc(consts_set, 1)

            pool.wait_ge(consts_set, 5)
            for c in range(2):
                pool.dma_start(sums[SEQ:SEQ + CAP, c * (D // 2):(c + 1) * (D // 2)].rearrange("p (c n) -> p c n", c=2),
                               zeros[:].unsqueeze(1).to_broadcast([CAP, 2, D // 4])).then_inc(sums_landed, 16)

            g.tensor_scalar(minus_from[:], minus_from[:], 0.0, -1.0, ALU.is_ge, ALU.mult).then_inc(bias_step, 1)
            for i in range(3):
                g.affine_select(out=part_of[:], in_=part_of[:], compare_op=ALU.not_equal, fill=1.0, base=-i * NE,
                                pattern=[[-1, NE + 1]], channel_multiplier=1).then_inc(bias_step, 1)
                pool.wait_ge(bias_step, 2 + i)
            pool.wait_ge(bias_in, 16 * 9)
            g.tensor_scalar(bias_raw[:, D:2 * D], bias_raw[:, D:2 * D], 1.0, None, ALU.add).then_inc(bias_step, 1)
            pool.wait_ge(bias_step, 5)
            for i in range(2):
                g.tensor_copy(bias_parts[:], bias_raw).then_inc(bias_step, 1)
                pool.wait_ge(bias_step, 6 + 3 * i)
                g.tensor_scalar(bias_parts[:], bias_parts[:], minus_from[:, 1 - i:2 - i], None, ALU.mult
                                ).then_inc(bias_step, 1)
                pool.wait_ge(bias_step, 7 + 3 * i)
                g.tensor_tensor(bias_raw, bias_raw, bias_parts[:], ALU.add).then_inc(bias_step, 1)
                pool.wait_ge(bias_step, 8 + 3 * i)
            g.tensor_copy(bias_parts[:], bias_raw).then_inc(parts_set, 1)

            pool.wait_ge(rounds_set, 1)
            rounds = pool.value_load(rounds_i[0:1, 0:1], min_val=1, max_val=ROUNDS)

            pool.wait_ge(normed_stored, 16)
            pool.wait_ge(sums_set, 16)

            def pace_step(i):
                g.tensor_tensor(pace[0:1, i:i + 1], steps[0:1, 0:1], steps[0:1, 0:1], ALU.add)

            def gather(j, I):
                pool.wait_ge(place_set, I + 1)
                pace_step(j % UNROLL)
                g.indirect_dma_start(out=x_rows[j % 2], out_offset=None, in_=normed_rows,
                                     in_offset=bass.IndirectOffsetOnAxis(ap=from_row[0:CAP, j % UNROLL:j % UNROLL + 1],
                                                                         axis=0)
                                     ).then_inc(gathered[j % 2], 16)

            def stage_bias(e, j):
                g.tensor_copy(bias_row[:, j % 2, :], part_of[:, bass.ds(e, 1)].to_broadcast([3 * NE, CAP])
                              ).then_inc(bias_set, 1)

            with pool.Fori(0, rounds) as r:
                gather(0, r * NEP)
                stage_bias(0, 0)
                gather(1, r * NEP + 1)
                with pool.Fori(0, BODIES) as b:
                    for j in range(UNROLL):
                        gather(j + AHEAD, r * NEP + b * UNROLL + (j + AHEAD))
                        stage_bias(b * UNROLL + (j + 1), j + 1)
                        A = r * NE + b * UNROLL + j
                        pool.wait_ge(y_scaled, A * 2 + 3)
                        pool.wait_ge(sums_landed, A * 16 + FIRST_SUMS)
                        pace_step(UNROLL + j)
                        g.indirect_dma_start(out=sums, out_offset=bass.IndirectOffsetOnAxis(
                                                 ap=to_row[0:CAP, j:j + 1], axis=0),
                                             in_=y_rows[j % 2], in_offset=None,
                                             compute_op=ALU.add).then_inc(sums_landed, 16)
                pool.wait_ge(bias_set, (r + 1) * (NE + 1))
                pace_step(2 * UNROLL)

        @block.scalar
        def _(act):
            s = nc.scalar
            b_in = a["b_in"][0]
            for row, n, src in (
                    (VG_MIX, 8, a["norm_mix_g"][0].rearrange("(k p) -> k p", p=P)),
                    (VG_FFN, 8, a["norm_ffn_g"][0].rearrange("(k p) -> k p", p=P)),
                    (VB_Q, 5, b_in[0:640].rearrange("(k p) -> k p", p=P)),
                    (VB_P, 4, b_in[768:1280].rearrange("(k p) -> k p", p=P)),
                    (V_SCALE, 4, a["pool_scale"][0].rearrange("(k p) -> k p", p=P))):
                act.dma_start(vec_rows[row:row + n, :], src).then_inc(vec_in, 16)
            for t in range(NT + 1):
                n = P if t < NT else META
                if t < NT:
                    act.wait_ge(x_in[t], 16)
                    s.activation(xn[:, t, :], hx[:, t, :], ACT.Square, accum_out=sq[:, t:t + 1]).then_inc(squared, 1)
                else:
                    act.wait_ge(meta_in, 16)
                    s.activation(meta_n, meta_x, ACT.Square, accum_out=sq[0:META, t:t + 1]).then_inc(squared, 1)
                act.wait_ge(var_set, t + 1)
                s.activation(rstd[0:n, t:t + 1], rstd[0:n, t:t + 1], ACT.Sqrt).then_inc(rooted, 1)

            act.dma_start(bv[:], b_in[640:768].partition_broadcast(P)).then_inc(consts_in, 16)
            act.dma_start(sinks[:], a["attn_sinks"][0].partition_broadcast(P)).then_inc(consts_in, 16)
            act.dma_start(b_router[:], a["b_router"][0].partition_broadcast(P)).then_inc(consts_in, 16)
            act.dma_start(w_router[:], a["w_router"][0].rearrange("(k p) n -> p k n", p=P)).then_inc(consts_in, 16)
            act.dma_start(w_pool, a["w_pool"][0].rearrange("g c e -> c g e")).then_inc(consts_in, 16)
            for i, name in enumerate(("b_gate", "b_up", "b_down")):
                for q in range(3):
                    act.dma_start(bias_raw[q * NE:(q + 1) * NE, i * D:(i + 1) * D], a[name][0]).then_inc(bias_in, 16)

            act.wait_ge(vecs_set, 1)
            act.wait_ge(proj, 1)
            s.activation(kT, bank[0][:, 0:SEQ], ACT.Identity, bias=col(VB_K, 1)).then_inc(proj_set, 1)
            act.wait_ge(proj, 2)
            s.activation(k_prev[:, 0, 64:PREV], bank[5][:, 0:META], ACT.Identity, bias=col(VB_K, 1))
            for c in range(NG):
                i = s.activation(pT[:, c, 0:META], bank[5][:, META * (1 + c):META * (2 + c)], ACT.Identity,
                                 bias=col(VB_P + c, 1))
            i.then_inc(proj_set, 1)
            for c in range(4):
                act.wait_ge(proj, 4 + c)
                s.activation(qT[:, c, :], bank[1 + c][:], ACT.Identity, bias=col(VB_Q + c, 1)).then_inc(proj_set, 1)

            for m in range(NT):
                act.wait_ge(max_set, m + 1)
                for h in range(HEADS):
                    s.activation(probs[:, h, :], bank[h // 2][:, (h % 2) * KEYS:(h % 2 + 1) * KEYS], ACT.Exp,
                                 bias=negm[:, h:h + 1], scale=SCALE, accum_out=den[:, h:h + 1])
                s.activation(sink_e[:], sink_e[:], ACT.Exp).then_inc(exp_set, 1)
                act.wait_ge(proj, 8 + m)
                s.activation(pT[:, m, META:], bank[4][:], ACT.Identity, bias=col(VB_P + m, 1)).then_inc(p_set, 1)
                for g in range(2):
                    act.wait_ge(probs_T, 2 * m + g + 1)
                    s.activation(probsT_own, bank[6 if g == 0 else 1][:].rearrange("p (h q) -> p h q", h=4),
                                 ACT.Copy).then_inc(probsT_set, 1)
            for g in range(NG):
                act.wait_ge(pooled, g + 1)
                s.activation(mixT[:, 4 + g, :], bank[2 + g][:], ACT.Copy, scale=col(V_SCALE + g, 1)).then_inc(pooled_set, 1)

            def high_part(u, A):
                for p in range(2):
                    if p == 0:
                        act.wait_ge(weights_in[u], A * 16 + 16)
                        act.wait_ge(high_used, A * 4 + (u + 1))
                    s.activation(half_unit(high_of[u % 2], p), half_unit(ring[u], p), ACT.Copy
                                 ).then_inc(high_set, 1)

            for t in range(NT):
                if t == NT - 1:
                    act.wait_ge(mixed, NT)
                    s.activation(den[:], den[:], ACT.Copy).then_inc(high_used, 2)
                    high_part(0, 0)
                act.wait_ge(h_set, t + 1)
                s.activation(normed[:, t, :], hx[:, t, :], ACT.Square, accum_out=sq[:, t:t + 1]).then_inc(squared, 1)
                act.wait_ge(var_set, 6 + t)
                s.activation(rstd[:, t:t + 1], rstd[:, t:t + 1], ACT.Sqrt).then_inc(rooted, 1)
            act.dma_start(sums[0:SEQ, :].rearrange("(t p) d -> p t d", p=P), hx[:]).then_inc(sums_set, 16)
            act.wait_ge(xn_set, 9)
            act.dma_start(normed_rows.rearrange("(t p) d -> p t d", p=P), normed[:, :, :]).then_inc(normed_stored, 16)
            high_part(1, 0)
            act.wait_ge(top_set, 1)
            s.activation(top_e[:], top_e[:], ACT.Exp).then_inc(top_exp, 1)

            s.activation(sink_e[:], sink_e[:], ACT.Copy).then_inc(y_scaled, 1)

            act.wait_ge(rounds_set, 1)
            rounds = act.value_load(rounds_i[0:1, 0:1], min_val=1, max_val=ROUNDS)
            with act.Fori(0, rounds) as r:
                with act.Fori(0, BODIES) as b:
                    for j in range(UNROLL):
                        A = r * NE + b * UNROLL + j

                        def sigmoid(h):
                            act.wait_ge(gate_capped, A * 2 + (h + 1))
                            s.activation(glu_t[:, h * COLS:(h + 1) * COLS], gate_t[:, h * COLS:(h + 1) * COLS],
                                         ACT.Sigmoid, scale=ALPHA).then_inc(sigmoids, 1)

                        def actT_out(h):
                            act.wait_ge(act_T, A * 2 + (h + 1))
                            s.activation(actT[:, 4 * h:4 * h + 4, :],
                                         bank[6 + h][:, 0:4 * CAP].rearrange("p (k n) -> p k n", k=4), ACT.Copy
                                         ).then_inc(actT_set, 1)

                        high_part(2, A)
                        sigmoid(0)
                        high_part(3, A)
                        actT_out(0)
                        high_part(0, A + 1)
                        sigmoid(1)
                        high_part(1, A + 1)
                        actT_out(1)
                        for h in range(2):
                            act.wait_ge(down_ready, A * 2 + (h + 1))
                            if h == 0:
                                act.wait_ge(sums_landed, A * 16 + FIRST_SUMS - 16)
                            s.activation(y_rows[j % 2][:, h * COLS:(h + 1) * COLS], bank[4 + h][0:CAP, :], ACT.Copy,
                                         scale=gate_c[0:CAP, j:j + 1]).then_inc(y_scaled, 1)

            for t in range(NT):
                act.wait_ge(final_in[t], 16)
                s.activation(normed[:, t, :], hx[:, t, :], ACT.Square, accum_out=sq[:, t:t + 1]).then_inc(squared, 1)
                act.wait_ge(var_set, 10 + t)
                s.activation(rstd[:, t:t + 1], rstd[:, t:t + 1], ACT.Sqrt).then_inc(rooted, 1)

        @block.vector
        def _(dve):
            v = nc.vector
            seq = [0]

            def then(ins):
                seq[0] += 1
                ins.then_inc(dve_seq, 1)
                dve.wait_ge(dve_seq, seq[0])

            def norm(t, done, src, dst, n=P, weight=None):
                dve.wait_ge(squared, done + 1)
                v.tensor_scalar(rstd[0:n, t:t + 1], sq[0:n, t:t + 1], 1.0 / D, EPS, ALU.mult, ALU.add).then_inc(var_set, 1)
                dve.wait_ge(rooted, done + 1)
                then(v.reciprocal(rstd[0:n, t:t + 1], rstd[0:n, t:t + 1]))
                if weight is not None:
                    v.scalar_tensor_tensor(out=dst, in0=src, scalar=rstd[0:n, t:t + 1], in1=weight, op0=ALU.mult,
                                           op1=ALU.mult).then_inc(out_set, 1)
                else:
                    v.tensor_scalar(dst, src, rstd[0:n, t:t + 1], None, ALU.mult).then_inc(xn_set, 1)

            v.memset(block_of[:], 0.0)
            then(v.memset(unseen[:], 0.0))
            for q in (0, 64):
                v.memset(block_of[q:q + 1, 0:64], 1.0)
                v.memset(block_of[q + 32:q + 33, 64:128], 1.0)
                v.memset(unseen[q:q + 1, :, PREV + 64:KEYS], NEG)
                v.memset(unseen[q + 32:q + 33, :, 0:64], NEG)
                v.memset(unseen[q:q + 1, 0, 0:64], NEG)
            dve.wait_ge(vecs_T, 1)
            v.tensor_copy(vec[:, 0:29], bank[7][:, 0:29]).then_inc(vecs_set, 1)
            dve.wait_ge(vecs_set, 1)

            def u_out(t):
                for h in range(2):
                    dve.wait_ge(u_T, 2 * t + h + 1)
                    v.tensor_tensor(uT[:, 4 * h:4 * h + 4, t * P:(t + 1) * P],
                                    bank[(2 * t + h) % 4][:].rearrange("p (k n) -> p k n", k=4),
                                    spread(col(VG_MIX + 4 * h, 4), P), ALU.mult).then_inc(u_set, 1)

            for t in range(NT):
                norm(t, t, hx[:, t, :], xn[:, t, :])
                if t:
                    u_out(t - 1)
            norm(NT, NT, meta_x, meta_n, META)
            u_out(NT - 1)
            dve.wait_ge(u_T, 2 * NT + 1)
            v.tensor_tensor(uT_meta, bank[4][:, 0:KC * META].rearrange("p (k n) -> p k n", k=KC),
                            spread(col(VG_MIX, KC), META), ALU.mult).then_inc(u_set, 1)

            v.memset(k_prev[:, 0, 0:64], 0.0)
            v.memset(v_prev[0:64, 0, :], 0.0)
            dve.wait_ge(proj_set, 2)
            for m in range(1, NT):
                v.tensor_copy(k_prev[:, m, 0:64], kT[:, m * P - 64:m * P])
                v.tensor_copy(k_prev[:, m, 64:PREV], k_prev[:, 0, 64:PREV])
            dve.wait_ge(proj, 3)
            dve.wait_ge(consts_in, 16 * 5)
            then(v.tensor_tensor(v_own, bank[6][:].rearrange("p (m n) -> p m n", m=NT),
                                 bv[:].unsqueeze(1).to_broadcast([P, NT, P]), ALU.add))
            for m in range(NT):
                v.tensor_tensor(v_prev[64:PREV, m, :], bank[5][0:META, 128:256], bv[0:META, :], ALU.add)
                if m:
                    i = v.tensor_copy(v_prev[0:64, m, :], v_own[64:128, m - 1, :])
            i.then_inc(v_set, 1)

            def pool_windows(g):
                dve.wait_ge(p_set, g + 1)
                src, w, lo = pT[:, g, :], 1, 0
                for i in range(g + 1):
                    dst = wsum[i % 2]
                    then(v.tensor_tensor(dst[:, lo + w:L], src[:, lo + w:L], src[:, lo:L - w], ALU.add))
                    src, lo, w = dst, lo + w, 2 * w
                v.scalar_tensor_tensor(out=diffT[:, g, :], in0=src[:, META:L], scalar=1.0 / POOL_WINDOWS[g],
                                       in1=pT[:, g, META:L], op0=ALU.mult, op1=ALU.subtract).then_inc(diff_set, 1)

            for m in range(NT):
                dve.wait_ge(scored, m + 1)
                for i in range(4):
                    ins = v.tensor_reduce(mx[:, 2 * i:2 * i + 2],
                                          bank[i][:, 0:2 * KEYS].rearrange("p (h k) -> p h k", h=2), AX.X, ALU.max)
                then(ins)
                then(v.scalar_tensor_tensor(out=mx[:], in0=mx[:], scalar=SCALE, in1=sinks[:], op0=ALU.mult, op1=ALU.max))
                if m:
                    dve.wait_ge(exp_set, m)
                v.tensor_tensor(sink_e[:], sinks[:], mx[:], ALU.subtract)
                v.tensor_scalar(negm[:], mx[:], -1.0, None, ALU.mult).then_inc(max_set, 1)
                if m:
                    pool_windows(m - 1)
                dve.wait_ge(exp_set, m + 1)
                then(v.tensor_tensor(den[:], den[:], sink_e[:], ALU.add))
                then(v.reciprocal(den[:], den[:]))
                v.tensor_tensor(probs[:], probs[:], spread(den[:], KEYS), ALU.mult).then_inc(probs_set, 1)
                for g in range(2):
                    dve.wait_ge(probs_T, 2 * m + g + 1)
                    v.tensor_copy(probsT_prev, bank[5 if g == 0 else 0][0:PREV, :].rearrange("p (h q) -> p h q", h=4)
                                  ).then_inc(probsT_set, 1)
                dve.wait_ge(attended, m + 1)
                v.tensor_copy(mixT[:, 0:4, m * P:(m + 1) * P], bank[7][:].rearrange("p (c q) -> p c q", c=4)
                              ).then_inc(mix_set, 1)

            pool_windows(NG - 1)

            def low_part(u, A, pieces=(0, 1)):
                for p in pieces:
                    dve.wait_ge(high_set, A * 8 + (2 * u + p + 1))
                    v.tensor_tensor(half_unit(ring_low[u], p), half_unit(ring[u], p), half_unit(high_of[u % 2], p),
                                    ALU.subtract).then_inc(low_set, 1)

            def residual(t):
                dve.wait_ge(mixed, t + 1)
                for h in range(2):
                    i = v.tensor_tensor(hx[:, t, h * 512:(h + 1) * 512], bank[2 * t + h][:],
                                        hx[:, t, h * 512:(h + 1) * 512], ALU.add)
                i.then_inc(h_set, 1)

            def f_out(t):
                for h in range(2):
                    dve.wait_ge(f_T, 2 * t + h + 1)
                    v.tensor_tensor(fT[:, 4 * h:4 * h + 4, t * P:(t + 1) * P],
                                    bank[2 * t + h][:].rearrange("p (k n) -> p k n", k=4),
                                    spread(col(VG_FFN + 4 * h, 4), P), ALU.mult).then_inc(f_set, 1)

            def top4(t):
                dve.wait_ge(routed, t + 1)
                then(v.tensor_tensor(logits[:, t, :], bank[2 * t][:, 0:NE], b_router[:], ALU.add))
                then(v.max(top[:, t, :], logits[:, t, :]))
                then(v.max_index(top_at[:, t, :], top[:, t, :], logits[:, t, :]))

            for t in range(NT):
                residual(t)
                norm(t, NT + 1 + t, hx[:, t, :], normed[:, t, :])
                if t == 1:
                    dve.wait_ge(parts_set, 1)
                if t:
                    f_out(t - 1)
                    top4(t - 1)
            low_part(0, 0)
            f_out(NT - 1)
            low_part(1, 0, (0,))
            top4(NT - 1)
            v.tensor_copy(top_f[:], top_at[:])
            v.tensor_tensor(top_e[:], top[:, :, 0:TOPK], top[:, :, 0:1].to_broadcast([P, NT, TOPK]),
                            ALU.subtract).then_inc(top_set, 1)
            low_part(1, 0, (1,))
            dve.wait_ge(top_exp, 1)
            then(v.tensor_reduce(top_s[:], top_e[:], AX.X, ALU.add))
            then(v.reciprocal(top_s[:], top_s[:]))
            then(v.tensor_tensor(top_e[:], top_e[:], spread(top_s[:], TOPK), ALU.mult))
            for t in range(NT):
                then(v.tensor_tensor(chosen[:], iota_exp[:].unsqueeze(1).to_broadcast([P, TOPK, NE]),
                                     spread(top_f[:, t, 0:TOPK], NE), ALU.is_equal))
                v.tensor_reduce(mask[:, t, :], chosen[:].rearrange("p k e -> p e k"), AX.X, ALU.add)
                then(v.tensor_tensor(chosen_g[:], chosen[:], spread(top_e[:, t, :], NE), ALU.mult))
                then(v.tensor_reduce(gates[:, t, :], chosen_g[:].rearrange("p k e -> p e k"), AX.X, ALU.add))
            v.tensor_copy(mask_b[:], mask[:]).then_inc(mask_set, 1)
            dve.wait_ge(mask_set, 1)
            then(v.tensor_scalar(mask[:], mask[:], FAR, CAP - FAR, ALU.mult, ALU.add))
            parts = gate_parts[:].rearrange("p t (e c) -> p t e c", c=3)
            then(v.memset(gate_parts[:], 0.0))
            for c in range(3):
                then(v.tensor_copy(parts[:, :, 0:NE, c], gates[:]))
                if c < 2:
                    then(v.tensor_tensor(gates[:], gates[:], parts[:, :, 0:NE, c], ALU.subtract))
            dve.wait_ge(ranked, 1)
            v.tensor_tensor(ranks[:, :, 0:NE], bank[2][:, 0:NT * NE].rearrange("p (t e) -> p t e", t=NT),
                            mask[:], ALU.add)
            then(v.tensor_reduce(count[:], bank[3][:, 0:NE], AX.X, ALU.max))
            then(v.tensor_scalar(over[:], steps[:], count[:], None, ALU.is_lt))
            then(v.tensor_reduce(rounds_f[:], over[:], AX.X, ALU.add))
            v.tensor_copy(rounds_i[:], rounds_f[:]).then_inc(rounds_set, 1)
            dve.wait_ge(rounds_set, 1)
            rounds = dve.value_load(rounds_i[0:1, 0:1], min_val=1, max_val=ROUNDS)

            def mark(e):
                v.tensor_tensor(hot[:], iota_cap[:].unsqueeze(1).to_broadcast([P, NT, CAP]),
                                ranks[:, :, bass.ds(e, 1)].to_broadcast([P, NT, CAP]), ALU.is_equal)
                v.tensor_copy(place_in[:, :, 2:5], gate_parts[:, :, bass.ds(e * 3, 3)]).then_inc(hot_set, 1)

            def places(j, I):
                dve.wait_ge(place_ready, I + 1)
                j = j % UNROLL
                src = bank[7][0:CAP, 4 * CAP:4 * CAP + 6]
                v.tensor_reduce(token_f[0:CAP], src[:, 0:2], AX.X, ALU.add)
                v.tensor_reduce(gate_c[0:CAP, j:j + 1], src[:, 2:5], AX.X, ALU.add)
                v.tensor_scalar(to_f[0:CAP], src[:, 5:6], spare[0:CAP, 1:2], spare[0:CAP, 0:1],
                                ALU.mult, ALU.add).then_inc(ranks_moved, 1)

            def places_end(j, n):
                dve.wait_ge(ranks_moved, n)
                j = j % UNROLL
                v.tensor_copy(from_row[0:CAP, j:j + 1], token_f[0:CAP])
                v.tensor_tensor(to_row[0:CAP, j:j + 1], to_f[0:CAP], token_f[0:CAP], ALU.add).then_inc(place_set, 1)

            def x_out(n):
                for h in range(2):
                    k = slice(4 * h, 4 * h + 4)
                    dve.wait_ge(x_T, n + h + 1)
                    v.tensor_tensor(x_f[:, k, :], bank[7 - h][:, 0:4 * CAP].rearrange("p (k n) -> p k n", k=4),
                                    spread(col(VG_FFN + 4 * h, 4), CAP), ALU.mult).then_inc(xf_set, 1)
                for h in range(2):
                    k = slice(4 * h, 4 * h + 4)
                    dve.wait_ge(xf_set, n + h + 1)
                    v.tensor_copy(x_high[:, k, :], x_f[:, k, :]).then_inc(xh_set, 1)
                for h in range(2):
                    k = slice(4 * h, 4 * h + 4)
                    dve.wait_ge(xh_set, n + h + 1)
                    v.tensor_tensor(x_low[:, k, :], x_f[:, k, :], x_high[:, k, :], ALU.subtract
                                    ).then_inc(xT_set, 1)

            dve.wait_ge(normed_stored, 16)
            with dve.Fori(0, rounds) as r:
                v.tensor_scalar(ranks[:], ranks[:], -float(CAP), None, ALU.add).then_inc(ranks_moved, 1)
                dve.wait_ge(ranks_moved, r * (NEP + 1) + 1)
                dve.wait_ge(sums_landed, r * (16 * NE) + FIRST_SUMS)
                for j in range(AHEAD):
                    mark(j)
                    places(j, r * NEP + j)
                    places_end(j, r * (NEP + 1) + (2 + j))
                x_out(r * (2 * (NE + 1)))
                with dve.Fori(0, BODIES) as b:
                    for j in range(UNROLL):
                        A = r * NE + b * UNROLL + j

                        def cap_gate(h):
                            dve.wait_ge(gate_ready, A * 2 + (h + 1))
                            v.tensor_scalar(gate_t[:, h * COLS:(h + 1) * COLS], bank[2 * h][0:CAP, :], LIMIT, None,
                                            ALU.min).then_inc(gate_capped, 1)

                        def activate(h):
                            c = slice(h * COLS, (h + 1) * COLS)
                            dve.wait_ge(sigmoids, A * 2 + (h + 1))
                            v.tensor_tensor(glu_t[:, c], gate_t[:, c], glu_t[:, c], ALU.mult).then_inc(glu_set, 1)
                            dve.wait_ge(up_ready, A * 2 + (h + 1))
                            v.tensor_scalar(up_t[:, c], bank[2 * h + 1][0:CAP, :], LIMIT + 1.0, None, ALU.min
                                            ).then_inc(up_capped, 1)
                            dve.wait_ge(up_capped, A * 2 + (h + 1))
                            v.scalar_tensor_tensor(out=act_t[:, c], in0=up_t[:, c], scalar=1.0 - LIMIT,
                                                   in1=glu_t[:, c], op0=ALU.max, op1=ALU.mult).then_inc(act_set, 1)

                        mark(b * UNROLL + (j + AHEAD))
                        cap_gate(0)
                        low_part(2, A)
                        activate(0)
                        low_part(3, A)
                        dve.wait_ge(sums_landed, A * 16 + FIRST_SUMS - 16)
                        places(j + AHEAD, r * NEP + b * UNROLL + (j + AHEAD))
                        places_end(j + AHEAD, r * (NEP + 1) + b * UNROLL + (j + AHEAD + 2))
                        cap_gate(1)
                        low_part(0, A + 1)
                        activate(1)
                        x_out((r * (NE + 1) + b * UNROLL + (j + 1)) * 2)
                        low_part(1, A + 1)

            for t in range(NT):
                dve.wait_ge(final_in[t], 16)
                if t == 0:
                    dve.wait_ge(g_final_in, 16)
                norm(t, 2 * NT + 1 + t, hx[:, t, :], normed[:, t, :], weight=g_final)

        @block.tensor
        def _(pe):
            mm = nc.tensor.matmul

            def tr(dst, src):
                return mm(dst, src, ident[0:src.shape[0], 0:src.shape[0]], start=True, stop=True, is_transpose=True)

            pe.wait_ge(consts_set, 2)
            pe.wait_ge(vec_in, 16 * 5)
            tr(bank[7][:, 0:29], vec_rows[0:29, :]).then_inc(vecs_T, 1)
            for t in range(NT):
                pe.wait_ge(xn_set, t + 1)
                if t >= 2:
                    pe.wait_ge(u_set, 2 * (t - 1))
                for h in range(2):
                    for k in range(4):
                        i = tr(bank[(2 * t + h) % 4][:, k * P:(k + 1) * P], xn[:, t, (4 * h + k) * P:(4 * h + k + 1) * P])
                    i.then_inc(u_T, 1)
            pe.wait_ge(xn_set, NT + 1)
            for k in range(KC):
                i = tr(bank[4][:, k * META:(k + 1) * META], meta_n[:, k * P:(k + 1) * P])
            i.then_inc(u_T, 1)
            pe.wait_ge(u_set, 2 * NT + 1)
            pe.wait_ge(vecs_set, 1)

            def project(dst, lhs, rhs):
                for k in range(KC):
                    i = mm(dst, lhs(k), rhs(k), start=k == 0, stop=k == KC - 1)
                return i

            pe.wait_ge(wkv_in, 16)
            project(bank[0][:, 0:SEQ], lambda k: wkv[:, k, 0:128], lambda k: uT[:, k, :]).then_inc(proj, 1)
            pe.wait_ge(wp_in, 16)
            project(bank[5][:, 0:META], lambda k: wkv[:, k, 0:128], lambda k: uT_meta[:, k, :])
            for c in range(NG):
                project(bank[5][:, META * (1 + c):META * (2 + c)], lambda k: wp[:, k, c * P:(c + 1) * P],
                        lambda k: uT_meta[:, k, :])
            project(bank[5][0:META, 128:256], lambda k: uT_meta[:, k, :], lambda k: wkv[:, k, 128:256]).then_inc(proj, 1)
            for m in range(NT):
                i = project(bank[6][:, m * P:(m + 1) * P], lambda k: uT[:, k, m * P:(m + 1) * P],
                            lambda k: wkv[:, k, 128:256])
            i.then_inc(proj, 1)
            pe.wait_ge(wq_in, 16)
            for c in range(4):
                project(bank[1 + c][:], lambda k: wq[:, k, c * P:(c + 1) * P], lambda k: uT[:, k, :]).then_inc(proj, 1)

            pe.wait_ge(proj_set, 6)
            pe.wait_ge(v_set, 1)
            for m in range(NT):
                if m:
                    pe.wait_ge(probsT_set, 4 * m)
                for h in range(HEADS):
                    g, c = divmod(h, HALF)
                    rows = slice(64 * g, 64 * g + 64)
                    dst = bank[h // 2][:, (h % 2) * KEYS:(h % 2 + 1) * KEYS]
                    q = qT[rows, c, m * P:(m + 1) * P]
                    mm(dst, block_of[rows, :], unseen[rows, min(m, 1), :], start=True, stop=False)
                    mm(dst[:, 0:PREV], q, k_prev[rows, m, :], start=False, stop=False)
                    i = mm(dst[:, PREV:KEYS], q, kT[rows, m * P:(m + 1) * P], start=False, stop=True)
                i.then_inc(scored, 1)
                if m:
                    pe.wait_ge(p_set, m)
                project(bank[4][:], lambda k: wp[:, k, m * P:(m + 1) * P], lambda k: uT[:, k, :]).then_inc(proj, 1)
                pe.wait_ge(probs_set, m + 1)
                for g in range(2):
                    prev, own = (bank[5], bank[6]) if g == 0 else (bank[0], bank[1])
                    for c in range(HALF):
                        tr(prev[0:PREV, c * P:(c + 1) * P], probs[:, HALF * g + c, 0:PREV])
                        i = tr(own[:, c * P:(c + 1) * P], probs[:, HALF * g + c, PREV:KEYS])
                    i.then_inc(probs_T, 1)
                    pe.wait_ge(probsT_set, 4 * m + 2 * g + 2)
                    if g == 0 and m:
                        pe.wait_ge(mix_set, m)
                    for c in range(HALF):
                        dst = bank[7][64 * g:64 * g + 64, c * P:(c + 1) * P]
                        mm(dst, v_prev[0:PREV, m, 64 * g:64 * g + 64], probsT_prev[:, c, :], start=True, stop=False)
                        i = mm(dst, v_own[:, m, 64 * g:64 * g + 64], probsT_own[:, c, :], start=False, stop=True)
                i.then_inc(attended, 1)

            for g in range(NG):
                pe.wait_ge(diff_set, g + 1)
                mm(bank[2 + g][:], w_pool[:, g, :], diffT[:, g, :], start=True, stop=True).then_inc(pooled, 1)

            pe.wait_ge(wout_in, 16 * 2)
            pe.wait_ge(mix_set, NT)

            def logits_of(t):
                pe.wait_ge(xn_set, NT + 2 + t)
                for h in range(2):
                    for k in range(4):
                        i = tr(bank[2 * t + h][:, k * P:(k + 1) * P],
                               normed[:, t, (4 * h + k) * P:(4 * h + k + 1) * P])
                    i.then_inc(f_T, 1)

            def route(t):
                pe.wait_ge(f_set, 2 * t + 2)
                project(bank[2 * t][:, 0:NE], lambda k: fT[:, k, t * P:(t + 1) * P],
                        lambda k: w_router[:, k, :]).then_inc(routed, 1)

            pe.wait_ge(pooled_set, NG)
            for t in range(NT):
                for h in range(2):
                    i = project(bank[2 * t + h][:], lambda k: mixT[:, k, t * P:(t + 1) * P], lambda k: wout[h][:, k, :])
                i.then_inc(mixed, 1)
                if t >= 1:
                    logits_of(t - 1)
                if t >= 2:
                    route(t - 2)
            logits_of(NT - 1)
            route(NT - 2)
            route(NT - 1)

            pe.wait_ge(mask_set, 1)
            for t in range(NT):
                dst = bank[2][:, t * NE:(t + 1) * NE]
                for q in range(t):
                    mm(dst, ones[:], mask_b[:, q, :], start=q == 0, stop=False)
                mm(dst, earlier[:], mask_b[:, t, :], start=t == 0, stop=True)
            for q in range(NT):
                i = mm(bank[3][:, 0:NE], ones[:], mask_b[:, q, :], start=q == 0, stop=q == NT - 1)
            i.then_inc(ranked, 1)

            pe.wait_ge(rounds_set, 1)
            rounds = pe.value_load(rounds_i[0:1, 0:1], min_val=1, max_val=ROUNDS)

            def find(I):
                pe.wait_ge(hot_set, I + 1)
                for t in range(NT):
                    i = mm(bank[7][0:CAP, 4 * CAP:4 * CAP + 6], hot[:, t, :], place_in[:, t, :],
                           start=t == 0, stop=t == NT - 1)
                i.then_inc(place_ready, 1)

            def x_transpose(j, G, I, first=None):
                pe.wait_ge(gathered[j % 2], G * 16 + 16)
                pe.wait_ge(place_set, I)
                for h in range(2):
                    if h and first is not None:
                        pe.wait_ge(actT_set, first)
                    for k in range(4):
                        i = tr(bank[7 - h][:, k * CAP:(k + 1) * CAP], x_rows[j % 2][:, (4 * h + k) * P:(4 * h + k + 1) * P])
                    i.then_inc(x_T, 1)

            per_round = NEP // 2
            with pe.Fori(0, rounds) as r:
                find(r * NEP)
                pe.wait_ge(place_set, r * NEP + 1)
                find(r * NEP + 1)
                x_transpose(0, r * per_round, r * NEP + 2)
                with pe.Fori(0, BODIES) as b:
                    for j in range(UNROLL):
                        A = r * NE + b * UNROLL + j
                        X = r * (NE + 1) + b * UNROLL + j
                        I = r * NEP + b * UNROLL + (j + AHEAD)

                        def bias(dst, kind, half):
                            c = kind * D + half * COLS
                            mm(dst, bias_row[:, j % 2, :], bias_parts[:, c:c + COLS], start=True, stop=False)

                        def act_transpose(h):
                            pe.wait_ge(act_set, A * 2 + (h + 1))
                            for k in range(4):
                                i = tr(bank[6 + h][:, k * CAP:(k + 1) * CAP],
                                       act_t[:, (4 * h + k) * P:(4 * h + k + 1) * P])
                            i.then_inc(act_T, 1)

                        def down(half, h):
                            for f in range(4 * half, 4 * half + 4):
                                i = mm(bank[4 + h][0:CAP, :], actT[:, f, :], slot[4 + h][:, f, :],
                                       start=False, stop=f == KC - 1)
                            if half:
                                i.then_inc(down_ready, 1)

                        pe.wait_ge(bias_set, X + 1)
                        pe.wait_ge(xT_set, X * 2 + 2)
                        for u in range(4):
                            half, kind = divmod(u, 2)
                            dst = bank[u][0:CAP, :]
                            bias(dst, kind, half)
                            w = high_of[kind][:].rearrange("p (k n) -> p k n", k=KC)
                            for k in range(KC):
                                if k % 4 == 0:
                                    pe.wait_ge(high_set, A * 8 + (2 * u + k // 4 + 1))
                                mm(dst, x_high[:, k, :], w[:, k, :], start=False, stop=False)
                                i = mm(dst, x_low[:, k, :], w[:, k, :], start=False, stop=False)
                            i.then_inc(high_used, 1)
                            w = ring_low[u][:].rearrange("p (k n) -> p k n", k=KC)
                            for k in range(KC):
                                if k % 4 == 0:
                                    pe.wait_ge(low_set, A * 8 + (2 * u + k // 4 + 1))
                                i = mm(dst, x_high[:, k, :], w[:, k, :], start=False, stop=k == KC - 1)
                            i.then_inc(up_ready if kind else gate_ready, 1)
                            if u == 0:
                                find(I)
                            if u == 2:
                                act_transpose(0)
                        x_transpose(j + 1, r * per_round + b * 2 + (j + 1) // 2, I + 1, A * 2 + 1)
                        pe.wait_ge(y_scaled, A * 2 + 1)
                        pe.wait_ge(weights_in[4], A * 16 + 16)
                        bias(bank[4][0:CAP, :], 2, 0)
                        down(0, 0)
                        pe.wait_ge(xf_set, X * 2 + 3)
                        act_transpose(1)
                        pe.wait_ge(weights_in[5], A * 16 + 16)
                        bias(bank[5][0:CAP, :], 2, 1)
                        down(0, 1)
                        pe.wait_ge(actT_set, A * 2 + 2)
                        down(1, 0)
                        down(1, 1)
                pe.wait_ge(gathered[1], (r * per_round + per_round) * 16)
                pe.wait_ge(xT_set, (r + 1) * (2 * (NE + 1)))


_SHAPE = (1, SEQ, D)


def kernel(**inputs):
    import numpy as _np
    import concourse.bacc as _bacc
    from concourse import mybir as _mybir
    from concourse.bass_utils import run_bass_kernel_spmd as _run

    nc = _bacc.Bacc("TRN2", target_bir_lowering=False, num_devices=1)
    def pairs(x, axis):
        at = [2 * h + g for g in range(2) for h in range(HALF)]
        order = _np.argsort(at)
        parts = _np.split(_np.asarray(x), [HEADS * HD], axis=axis)
        heads = _np.split(parts[0], HEADS, axis=axis)
        return _np.concatenate([heads[i] for i in order] + [parts[1]], axis=axis)

    inputs = dict(inputs, w_in=pairs(inputs["w_in"], 2), b_in=pairs(inputs["b_in"], 1),
                  w_out=pairs(inputs["w_out"], 1))
    arrays, args = {}, {}
    for name, x in inputs.items():
        x = _np.ascontiguousarray(x)
        arrays[f"in_{name}"] = x
        args[name] = nc.dram_tensor(f"in_{name}", x.shape, _mybir.dt.from_np(x.dtype), kind="ExternalInput").ap()
    out = nc.dram_tensor("out_0", _SHAPE, _mybir.dt.float32, kind="ExternalOutput").ap()
    build(nc, args, out)
    r = _run(nc, [arrays], core_ids=[0])
    return r.results[0]["out_0"]
```

```python
from contextlib import ExitStack

import concourse.bass as bass
from concourse import mybir

F32 = mybir.dt.float32
BF16 = mybir.dt.bfloat16
F32R = mybir.dt.float32r
U32 = mybir.dt.uint32
I32 = mybir.dt.int32
ALU = mybir.AluOpType
ACT = mybir.ActivationFunctionType
AX = mybir.AxisListType

P = 128
D = 1024
KC = D // P
SEQ = 512
NT = SEQ // P
META = 16
HD = 64
SCALE = HD ** -0.5
HEADS = 8
HALF = HEADS // 2
PREV = 64 + META
KEYS = PREV + P
NG = 4
POOL_WINDOWS = (2, 4, 8, 16)
NE = 32
TOPK = 4
CAP = 96
ROUNDS = -(-SEQ // CAP)
LIMIT, ALPHA = 7.0, 1.702
EPS = 1e-5
NEG = -1e30
FAR = 1.0e6
UNROLL = 4
BODIES = NE // UNROLL
SPLIT = 5
UNITS = 6
COLS = 512
AHEAD = 2
NEP = NE + AHEAD
FIRST_SUMS = 32


def build(nc, a, out):
    ctx = ExitStack()
    with ctx:
        def sb(name, shape, dt=F32):
            return ctx.enter_context(nc.sbuf_tensor(name, shape, dt))

        def lent(name, shape, dt=F32):
            with nc.sbuf_tensor(name, shape, dt) as t:
                return t

        def sem(name):
            return ctx.enter_context(nc.semaphore(name))

        normed_rows = nc.dram_tensor("normed_rows", (SEQ, D), F32).ap()
        sums = nc.dram_tensor("sums", (SEQ + CAP, D), F32).ap()

        ring = []
        ring_low = []
        for u in range(UNITS):
            if u < SPLIT:
                ring.append(lent(f"ring{u}", [P, KC * COLS]))
                ring_low.append(sb(f"ring_low{u}", [P, KC * COLS], F32R))
            else:
                ring.append(sb(f"ring{u}", [P, KC * COLS]))
        wout_rows, high_of = [], []
        for h in range(2):
            wout_rows.append(lent(f"wout{h}", [P, KC * COLS]))
            high_of.append(sb(f"high_of{h}", [P, KC * COLS], F32R))
        slot = [r[:].rearrange("p (k n) -> p k n", k=KC) for r in ring]
        uT = ring[0][:].rearrange("p (k n) -> p k n", k=KC)
        qT = ring[1][:, 0:4 * SEQ].rearrange("p (c n) -> p c n", c=4)
        diffT = ring[1][:, 4 * SEQ:8 * SEQ].rearrange("p (c n) -> p c n", c=4)
        probs = ring[2][:, 0:HEADS * KEYS].rearrange("p (h k) -> p h k", h=HEADS)
        o = HEADS * KEYS
        probsT_rows = [ring[2][:, o:o + 1024]]
        o += 1024
        L = META + SEQ
        wsum = [ring[2][:, o + i * L:o + (i + 1) * L] for i in range(2)]
        wq, wp = slot[3], slot[4]
        wkv = ring[5][:, 0:KC * 256].rearrange("p (k n) -> p k n", k=KC)
        o = KC * 256
        kT = ring[5][:, o:o + SEQ]
        o += SEQ
        k_prev = ring[5][:, o:o + NT * PREV].rearrange("p (m k) -> p m k", m=NT)
        o += NT * PREV
        v_own = ring[5][:, o:o + NT * P].rearrange("p (m n) -> p m n", m=NT)
        o += NT * P
        v_prev = ring[5][:, o:o + NT * P].rearrange("p (m n) -> p m n", m=NT)
        wout = [h[:].rearrange("p (k n) -> p k n", k=KC) for h in wout_rows]

        hx = sb("hx", [P, NT, D])
        work_0 = lent("work_0", [P, KC * SEQ])
        wp_high = lent("wp_high", [P, KC * SEQ], F32R)
        rows_0 = sb("rows_0", [P, KC * SEQ])
        work_1 = lent("work_1", [P, KC * SEQ])
        rows_1 = sb("rows_1", [P, KC * SEQ - 2 * KC * CAP])
        act_split = sb("act_split", [P, 2 * KC * CAP], F32R)
        work_2 = lent("work_2", [P, KC * SEQ])
        x_split = sb("x_split", [P, 2 * KC * CAP], F32R)
        y_both = sb("y_both", [CAP, 2 * D])
        gate_parts = sb("gate_parts", [P, NT, 3 * NEP], BF16)
        hot = sb("hot", [P, NT, CAP], BF16)
        left = KC * SEQ - 2 * KC * CAP - 2 * D - NT * (3 * NEP + CAP) // 2
        assert left >= 0
        sb("work_2_end", [P, left])
        third = [work_0[:], work_1[:], work_2[:]]
        xn = third[0].rearrange("p (t d) -> p t d", t=NT)
        mixT = slot[3]
        normed = third[1].rearrange("p (t d) -> p t d", t=NT)
        pT = third[1][:, 0:NG * L].rearrange("p (g n) -> p g n", g=NG)
        meta_x = third[1][0:META, NG * L:NG * L + D]
        vec_rows = third[1][0:32, NG * L + D:NG * L + D + P]
        bias_raw = third[2][0:3 * NE, 0:3 * D]
        meta_n = third[2][0:META, 3 * D:4 * D]
        probsT_rows.append(third[2][:, 3 * D:4 * D])
        probsT_prev = [r[0:PREV, 0:512].rearrange("p (h q) -> p h q", h=4) for r in probsT_rows]
        probsT_own = [r[:, 512:1024].rearrange("p (h q) -> p h q", h=4) for r in probsT_rows]
        fT = third[2].rearrange("p (k n) -> p k n", k=KC)
        parts_of = [(high_of[0], ring[0], high_of[1]),
                    (ring_low[2], ring[3], ring_low[3]),
                    (wp_high, ring[4], ring_low[4])]
        u_parts, wq_parts, wp_parts = (
            [x[:].rearrange("p (k n) -> p k n", k=KC) for x in (high, low)] for high, _, low in parts_of)
        x_rows = [rows_0[0:CAP, i * D:(i + 1) * D] for i in range(2)]
        gate_t, glu_t = (rows_0[0:CAP, i * D:(i + 1) * D] for i in range(2, 4))
        up_t = act_t = rows_1[0:CAP, 0:D]
        o = D
        x_f = rows_1[:, o:o + KC * CAP].rearrange("p (k n) -> p k n", k=KC)
        o += KC * CAP
        actT = rows_1[:, o:o + KC * CAP].rearrange("p (k n) -> p k n", k=KC)
        x_high, x_low = (x_split[:, i * KC * CAP:(i + 1) * KC * CAP].rearrange("p (k n) -> p k n", k=KC)
                         for i in range(2))
        act_high, act_low = (act_split[:, i * KC * CAP:(i + 1) * KC * CAP].rearrange("p (k n) -> p k n", k=KC)
                             for i in range(2))
        y_rows = [y_both[:, i * D:(i + 1) * D] for i in range(2)]
        g_final = ring[2][:, 0:D]

        ident = sb("ident", [P, P])
        iota_cap = sb("iota_cap", [P, CAP])
        iota_exp = sb("iota_exp", [P, NE])
        steps = sb("steps", [P, ROUNDS])
        earlier = sb("earlier", [P, P], BF16)
        ones = sb("ones", [P, P], BF16)
        block_of = sb("block_of", [P, P], BF16)
        unseen = sb("unseen", [P, 2, KEYS], BF16)
        pace = sb("pace", [1, 2 * UNROLL + 1])
        zeros = sb("zeros", [CAP, D // 4])
        spare = sb("spare", [P, 2])
        place_in = sb("place_in", [P, NT, 6], BF16)
        vec = sb("vec", [P, 32])
        VG_MIX, VG_FFN, VB_Q, VB_K, VB_P, V_SCALE = 0, 8, 16, 20, 21, 25
        sinks = sb("sinks", [P, HEADS])
        b_router = sb("b_router", [P, NE])
        w_router = sb("w_router", [P, KC, NE])
        o = NG * L + D + P
        w_pool = third[1][:, o:o + NG * P].rearrange("p (g n) -> p g n", g=NG)
        o += NG * P
        uT_meta = third[1][:, o:o + KC * META].rearrange("p (k n) -> p k n", k=KC)
        o += KC * META
        bv = third[1][:, o:o + P]
        sq = sb("sq", [P, 5])
        rstd = sb("rstd", [P, 5])
        mx = sb("mx", [P, HEADS])
        negm = sb("negm", [P, HEADS])
        sink_e = sb("sink_e", [P, HEADS])
        den = sb("den", [P, HEADS])
        logits = sb("logits", [P, NT, NE])
        top = sb("top", [P, NT, 8])
        top_at = sb("top_at", [P, NT, 8], U32)
        top_f = sb("top_f", [P, NT, 8])
        top_e = sb("top_e", [P, NT, TOPK])
        top_s = sb("top_s", [P, NT])
        chosen, chosen_g = (third[2][:, i * NT * TOPK * NE:(i + 1) * NT * TOPK * NE].rearrange(
            "p (t k e) -> p t k e", t=NT, k=TOPK) for i in range(2))
        mask = sb("mask", [P, NT, NE])
        mask_b = sb("mask_b", [P, NT, NE], BF16)
        ranks = sb("ranks", [P, NT, NEP])
        gates = logits
        count = sb("count", [P, 1])
        over = sb("over", [P, ROUNDS])
        rounds_f = sb("rounds_f", [P, 1])
        rounds_i = sb("rounds_i", [P, 1], I32)
        bias_parts = sb("bias_parts", [3 * NE, 3 * D], BF16)
        part_of = sb("part_of", [3 * NE, NE + 1], BF16)
        bias_row = sb("bias_row", [3 * NE, 2, CAP], BF16)
        minus_from = sb("minus_from", [3 * NE, 2])
        from_row = sb("from_row", [P, UNROLL], U32)
        to_row = sb("to_row", [P, UNROLL], U32)
        to_f = sb("to_f", [P, 1])
        token_f = sb("token_f", [P, 1])
        gate_c = sb("gate_c", [P, UNROLL])

        bank = [ctx.enter_context(nc.psum_tensor(f"bank{i}", [P, 512], F32)) for i in range(8)]

        x_in = [sem(f"x_in{t}") for t in range(NT)]
        meta_in, vec_in, consts_in = sem("meta_in"), sem("vec_in"), sem("consts_in")
        wkv_in, wq_in, wp_in, wout_in = sem("wkv_in"), sem("wq_in"), sem("wp_in"), [sem(f"wout_in{h}") for h in range(2)]
        weights_in = [sem(f"weights_in{i}") for i in range(UNITS)]
        consts_set = sem("consts_set")
        squared, rooted, var_set, xn_set = sem("squared"), sem("rooted"), sem("var_set"), sem("xn_set")
        vecs_T, vecs_set = sem("vecs_T"), sem("vecs_set")
        u_T, u_set = sem("u_T"), sem("u_set")
        proj, proj_set = sem("proj"), sem("proj_set")
        v_set = sem("v_set")
        scored, max_set, exp_set, probs_set = sem("scored"), sem("max_set"), sem("exp_set"), sem("probs_set")
        probs_T, probsT_set = sem("probs_T"), [sem(f"probsT_set{g}") for g in range(2)]
        attended, mix_set = sem("attended"), sem("mix_set")
        diff_set, pooled, pooled_set = sem("diff_set"), sem("pooled"), sem("pooled_set")
        p_set = sem("p_set")
        split_high, split_low = sem("split_high"), sem("split_low")
        mixed, h_set, f_T, f_set, routed, logits_set = (
            sem("mixed"), sem("h_set"), sem("f_T"), sem("f_set"), sem("routed"), sem("logits_set"))
        top_set, top_exp = sem("top_set"), sem("top_exp")
        mask_set, ranked, rounds_set = sem("mask_set"), sem("ranked"), sem("rounds_set")
        normed_stored = sem("normed_stored")
        sums_set = sem("sums_set")
        g_final_in = sem("g_final_in")
        dve_seq = sem("dve_seq")
        ranks_moved, hot_set, place_ready, place_set = (
            sem("ranks_moved"), sem("hot_set"), sem("place_ready"), sem("place_set"))
        gathered = [sem(f"gathered{i}") for i in range(2)]
        x_T, xf_set, xh_set, xT_set, bias_set = (
            sem("x_T"), sem("xf_set"), sem("xh_set"), sem("xT_set"), sem("bias_set"))
        high_set, low_set, high_used = sem("high_set"), sem("low_set"), sem("high_used")
        gate_ready, gate_capped, sigmoids = sem("gate_ready"), sem("gate_capped"), sem("sigmoids")
        up_ready, up_capped, glu_set, act_set = sem("up_ready"), sem("up_capped"), sem("glu_set"), sem("act_set")
        act_T, actT_set, act_low_set = sem("act_T"), sem("actT_set"), sem("act_low_set")
        down_ready, y_scaled = sem("down_ready"), sem("y_scaled")
        bias_in, bias_step, parts_set = sem("bias_in"), sem("bias_step"), sem("parts_set")
        sums_landed = sem("sums_landed")
        final_in = [sem(f"final_in{t}") for t in range(NT)]
        out_set, stored = sem("out_set"), sem("stored")

        def col(v, n):
            return vec[:, v:v + n]

        def spread(ap, n):
            return ap.unsqueeze(2).to_broadcast([ap.shape[0], ap.shape[1], n])

        weight = [a["w_gate"], a["w_up"], a["w_gate"], a["w_up"], a["w_down"], a["w_down"]]
        which_half = [0, 0, 1, 1, 0, 1]

        def unit_src(at, u):
            c = which_half[u] * COLS
            whole = weight[u][0].rearrange("e d n -> (e d n)")
            return whole[bass.ds(at, D * D)].rearrange("(k p n) -> p k n", p=P, n=D)[:, :, c:c + COLS]

        def half_unit(ap, p):
            return ap[:, p * (KC // 2) * COLS:(p + 1) * (KC // 2) * COLS]

        block = ctx.enter_context(nc.Block())

        @block.sync
        def _(sp):
            xr = a["x"][0].rearrange("(t p) d -> p t d", p=P)
            for t in range(NT):
                sp.dma_start(hx[:, t, :], xr[:, t, :]).then_inc(x_in[t], 16)
                if t == 0:
                    b_in = a["b_in"][0]
                    for row, n, src in (
                            (VG_MIX, 8, a["norm_mix_g"][0].rearrange("(k p) -> k p", p=P)),
                            (VG_FFN, 8, a["norm_ffn_g"][0].rearrange("(k p) -> k p", p=P)),
                            (VB_Q, 5, b_in[0:640].rearrange("(k p) -> k p", p=P)),
                            (VB_P, 4, b_in[768:1280].rearrange("(k p) -> k p", p=P)),
                            (V_SCALE, 4, a["pool_scale"][0].rearrange("(k p) -> k p", p=P))):
                        sp.dma_start(vec_rows[row:row + n, :], src).then_inc(vec_in, 16)
            sp.dma_start(meta_x, a["meta_tokens"]).then_inc(meta_in, 16)
            w_in = a["w_in"][0].rearrange("(k p) n -> p k n", p=P)
            sp.dma_start(wkv, w_in[:, :, 512:768]).then_inc(wkv_in, 16)
            sp.dma_start(wq, w_in[:, :, 0:512]).then_inc(wq_in, 16)
            sp.dma_start(wp, w_in[:, :, 768:1280]).then_inc(wp_in, 16)
            w_out = a["w_out"][0].rearrange("(k p) n -> p k n", p=P)
            start = sp.alloc_register("unit_start")

            def load(e, u, wait=None):
                if wait is not None:
                    sp.reg_mul(start, e, D * D)
                    sp.reg_sub(start, start, COLS)
                    at = sp.snap(start, min_val=D * D - COLS, max_val=(NE - 1) * D * D - COLS) + COLS
                    freed(u, wait)
                else:
                    at = e * D * D
                sp.dma_start(slot[u], unit_src(at, u)).then_inc(weights_in[u], 16)

            def freed(u, A):
                if u >= 4:
                    sp.wait_ge(down_ready, A * 2 + (6 - u))
                else:
                    sp.wait_ge(gate_ready if u % 2 == 0 else up_ready, A * 2 + (1 + u // 2))

            sp.wait_ge(proj, 7 + NG)
            for h in range(2):
                sp.dma_start(wout[h], w_out[:, :, h * COLS:(h + 1) * COLS]).then_inc(wout_in[h], 16)
            for u in (0, 4):
                load(0, u)
            sp.wait_ge(pooled, NG)
            for u in (1, 2, 5):
                load(0, u)
            sp.wait_ge(mixed, NT)
            load(0, 3)

            sp.wait_ge(rounds_set, 1)
            rounds = sp.value_load(rounds_i[0:1, 0:1], min_val=1, max_val=ROUNDS)
            with sp.Fori(0, rounds) as r:
                with sp.Fori(0, NE - 1) as e:
                    for u in range(UNITS):
                        load(e + 1, u, r * NE + e)
                for u in range(2):
                    freed(u, r * NE + (NE - 1))
                    load(0, u)
                with sp.If(r + 1 < rounds):
                    for u in range(2, UNITS):
                        freed(u, r * NE + (NE - 1))
                        load(0, u)

            sp.wait_ge(up_ready, rounds * (2 * NE))
            sp.dma_start(g_final, a["norm_final_g"].partition_broadcast(P)).then_inc(g_final_in, 16)
            sp.wait_ge(sums_landed, rounds * (16 * NE) + FIRST_SUMS)
            sr = sums[0:SEQ, :].rearrange("(t p) d -> p t d", p=P)
            for t in range(NT):
                sp.dma_start(hx[:, t, :], sr[:, t, :]).then_inc(final_in[t], 16)
            outr = out[0].rearrange("(t p) d -> p t d", p=P)
            for t in range(NT):
                sp.wait_ge(out_set, t + 1)
                sp.dma_start(outr[:, t, :], normed[:, t, :]).then_inc(stored, 16)
            sp.wait_ge(stored, 16 * NT)

        @block.gpsimd
        def _(pool):
            g = nc.gpsimd
            g.memset(ident[:], 0.0).then_inc(consts_set, 1)
            pool.wait_ge(consts_set, 1)
            g.affine_select(out=ident[:], in_=ident[:], compare_op=ALU.not_equal, fill=1.0, base=0,
                            pattern=[[-1, P]], channel_multiplier=1).then_inc(consts_set, 1)
            g.memset(earlier[:], 1.0).then_inc(consts_set, 1)
            pool.wait_ge(consts_set, 3)
            g.affine_select(out=earlier[:], in_=earlier[:], compare_op=ALU.is_gt, fill=0.0, base=0,
                            pattern=[[1, P]], channel_multiplier=-1)
            g.memset(ones[:], 1.0)
            g.memset(zeros[:], 0.0)
            g.iota(iota_cap[:], pattern=[[1, CAP]], base=0, channel_multiplier=0, allow_small_or_imprecise_dtypes=True)
            g.iota(iota_exp[:], pattern=[[1, NE]], base=0, channel_multiplier=0, allow_small_or_imprecise_dtypes=True)
            g.iota(steps[:], pattern=[[CAP, ROUNDS]], base=0, channel_multiplier=0, allow_small_or_imprecise_dtypes=True)
            g.iota(spare[:, 0:1], pattern=[[1, 1]], base=SEQ, channel_multiplier=1, allow_small_or_imprecise_dtypes=True)
            g.iota(spare[:, 1:2], pattern=[[1, 1]], base=-SEQ, channel_multiplier=-1, allow_small_or_imprecise_dtypes=True)
            g.memset(place_in[:], 1.0).then_inc(consts_set, 1)
            pool.wait_ge(consts_set, 4)
            g.iota(place_in[:, :, 0:1], pattern=[[0, NT], [0, 1]], base=0, channel_multiplier=1,
                   allow_small_or_imprecise_dtypes=True)
            g.iota(place_in[:, :, 1:2], pattern=[[P, NT], [0, 1]], base=0, channel_multiplier=0,
                   allow_small_or_imprecise_dtypes=True)
            g.memset(ranks[:], -FAR)
            g.memset(part_of[:], 0.0)
            g.iota(minus_from[:], pattern=[[NE, 2]], base=-2 * NE, channel_multiplier=1,
                   allow_small_or_imprecise_dtypes=True).then_inc(consts_set, 1)

            pool.wait_ge(consts_set, 5)
            for c in range(2):
                pool.dma_start(sums[SEQ:SEQ + CAP, c * (D // 2):(c + 1) * (D // 2)].rearrange("p (c n) -> p c n", c=2),
                               zeros[:].unsqueeze(1).to_broadcast([CAP, 2, D // 4])).then_inc(sums_landed, 16)

            g.tensor_scalar(minus_from[:], minus_from[:], 0.0, -1.0, ALU.is_ge, ALU.mult).then_inc(bias_step, 1)
            for i in range(3):
                g.affine_select(out=part_of[:], in_=part_of[:], compare_op=ALU.not_equal, fill=1.0, base=-i * NE,
                                pattern=[[-1, NE + 1]], channel_multiplier=1).then_inc(bias_step, 1)
                pool.wait_ge(bias_step, 2 + i)
            pool.wait_ge(bias_in, 16 * 9)
            g.tensor_scalar(bias_raw[:, D:2 * D], bias_raw[:, D:2 * D], 1.0, None, ALU.add).then_inc(bias_step, 1)
            pool.wait_ge(bias_step, 5)
            for i in range(2):
                g.tensor_copy(bias_parts[:], bias_raw).then_inc(bias_step, 1)
                pool.wait_ge(bias_step, 6 + 3 * i)
                g.tensor_scalar(bias_parts[:], bias_parts[:], minus_from[:, 1 - i:2 - i], None, ALU.mult
                                ).then_inc(bias_step, 1)
                pool.wait_ge(bias_step, 7 + 3 * i)
                g.tensor_tensor(bias_raw, bias_raw, bias_parts[:], ALU.add).then_inc(bias_step, 1)
                pool.wait_ge(bias_step, 8 + 3 * i)
            g.tensor_copy(bias_parts[:], bias_raw).then_inc(parts_set, 1)

            pool.wait_ge(low_set, 2)
            for p in range(2):
                pool.wait_ge(high_set, 3 + p)
                g.tensor_tensor(half_unit(ring_low[1], p), half_unit(ring[1], p), half_unit(high_of[1], p), ALU.subtract
                                ).then_inc(low_set, 1)

            pool.wait_ge(rounds_set, 1)
            rounds = pool.value_load(rounds_i[0:1, 0:1], min_val=1, max_val=ROUNDS)

            pool.wait_ge(normed_stored, 16)
            pool.wait_ge(sums_set, 16)

            def pace_step(i):
                g.tensor_tensor(pace[0:1, i:i + 1], steps[0:1, 0:1], steps[0:1, 0:1], ALU.add)

            def gather(j, I):
                pool.wait_ge(place_set, I + 1)
                pace_step(j % UNROLL)
                g.indirect_dma_start(out=x_rows[j % 2], out_offset=None, in_=normed_rows,
                                     in_offset=bass.IndirectOffsetOnAxis(ap=from_row[0:CAP, j % UNROLL:j % UNROLL + 1],
                                                                         axis=0)
                                     ).then_inc(gathered[j % 2], 16)

            def stage_bias(e, j):
                g.tensor_copy(bias_row[:, j % 2, :], part_of[:, bass.ds(e, 1)].to_broadcast([3 * NE, CAP])
                              ).then_inc(bias_set, 1)

            with pool.Fori(0, rounds) as r:
                gather(0, r * NEP)
                stage_bias(0, 0)
                gather(1, r * NEP + 1)
                with pool.Fori(0, BODIES) as b:
                    for j in range(UNROLL):
                        gather(j + AHEAD, r * NEP + b * UNROLL + (j + AHEAD))
                        stage_bias(b * UNROLL + (j + 1), j + 1)
                        A = r * NE + b * UNROLL + j
                        pool.wait_ge(y_scaled, A * 2 + 3)
                        pool.wait_ge(sums_landed, A * 16 + FIRST_SUMS)
                        pace_step(UNROLL + j)
                        g.indirect_dma_start(out=sums, out_offset=bass.IndirectOffsetOnAxis(
                                                 ap=to_row[0:CAP, j:j + 1], axis=0),
                                             in_=y_rows[j % 2], in_offset=None,
                                             compute_op=ALU.add).then_inc(sums_landed, 16)
                pool.wait_ge(bias_set, (r + 1) * (NE + 1))
                pace_step(2 * UNROLL)

        @block.scalar
        def _(act):
            s = nc.scalar
            for t in range(NT + 1):
                n = P if t < NT else META
                if t < NT:
                    act.wait_ge(x_in[t], 16)
                    s.activation(xn[:, t, :], hx[:, t, :], ACT.Square, accum_out=sq[:, t:t + 1]).then_inc(squared, 1)
                else:
                    act.wait_ge(meta_in, 16)
                    s.activation(meta_n, meta_x, ACT.Square, accum_out=sq[0:META, t:t + 1]).then_inc(squared, 1)
                act.wait_ge(var_set, t + 1)
                s.activation(rstd[0:n, t:t + 1], rstd[0:n, t:t + 1], ACT.Sqrt).then_inc(rooted, 1)

            b_in = a["b_in"][0]
            act.dma_start(bv, b_in[640:768].partition_broadcast(P)).then_inc(consts_in, 16)
            act.dma_start(sinks[:], a["attn_sinks"][0].partition_broadcast(P)).then_inc(consts_in, 16)
            act.dma_start(b_router[:], a["b_router"][0].partition_broadcast(P)).then_inc(consts_in, 16)
            act.dma_start(w_router[:], a["w_router"][0].rearrange("(k p) n -> p k n", p=P)).then_inc(consts_in, 16)
            act.dma_start(w_pool, a["w_pool"][0].rearrange("g c e -> c g e")).then_inc(consts_in, 16)
            for i, name in enumerate(("b_gate", "b_up", "b_down")):
                for q in range(3):
                    act.dma_start(bias_raw[q * NE:(q + 1) * NE, i * D:(i + 1) * D], a[name][0]).then_inc(bias_in, 16)

            def split_high_part(i):
                high, whole, _ = parts_of[i]
                for p in range(2):
                    s.activation(half_unit(high, p), half_unit(whole, p), ACT.Copy).then_inc(split_high, 1)

            act.wait_ge(u_set, 2 * NT)
            split_high_part(0)
            act.wait_ge(wq_in, 16)
            split_high_part(1)

            act.wait_ge(vecs_set, 1)
            act.wait_ge(proj, 1)
            s.activation(kT, bank[0][:, 0:SEQ], ACT.Identity, bias=col(VB_K, 1)).then_inc(proj_set, 1)
            act.wait_ge(proj, 2)
            s.activation(k_prev[:, 0, 64:PREV], bank[5][:, 0:META], ACT.Identity, bias=col(VB_K, 1))
            for c in range(NG):
                i = s.activation(pT[:, c, 0:META], bank[5][:, META * (1 + c):META * (2 + c)], ACT.Identity,
                                 bias=col(VB_P + c, 1))
            i.then_inc(proj_set, 1)
            split_high_part(2)
            for c in range(4):
                act.wait_ge(proj, 4 + c)
                s.activation(qT[:, c, :], bank[1 + c][:], ACT.Identity, bias=col(VB_Q + c, 1)).then_inc(proj_set, 1)

            for m in range(NT):
                for g in range(2):
                    act.wait_ge(max_set, 2 * m + g + 1)
                    for h in range(HALF * g, HALF * g + HALF):
                        s.activation(probs[:, h, :], bank[h // 2][:, (h % 2) * KEYS:(h % 2 + 1) * KEYS], ACT.Exp,
                                     bias=negm[:, h:h + 1], scale=SCALE, accum_out=den[:, h:h + 1])
                    heads = slice(HALF * g, HALF * g + HALF)
                    s.activation(sink_e[:, heads], sink_e[:, heads], ACT.Exp).then_inc(exp_set, 1)
                act.wait_ge(proj, 8 + m)
                s.activation(pT[:, m, META:], bank[4][:], ACT.Identity, bias=col(VB_P + m, 1)).then_inc(p_set, 1)
                for g in range(2):
                    act.wait_ge(probs_T, 2 * m + g + 1)
                    s.activation(probsT_own[g], bank[6 if g == 0 else 1][:].rearrange("p (h q) -> p h q", h=4),
                                 ACT.Copy).then_inc(probsT_set[g], 1)
            for g in range(NG):
                act.wait_ge(pooled, g + 1)
                s.activation(mixT[:, 4 + g, :], bank[2 + g][:], ACT.Copy, scale=col(V_SCALE + g, 1)).then_inc(pooled_set, 1)

            def high_part(u, A, buffer, first=False):
                for p in range(2):
                    if p == 0:
                        act.wait_ge(weights_in[u], A * 16 + 16)
                        act.wait_ge(high_used, A * SPLIT + (u + 1))
                        if not first:
                            act.wait_ge(low_set, A * (2 * SPLIT) + (2 * u - 2))
                    s.activation(half_unit(high_of[buffer], p), half_unit(ring[u], p), ACT.Copy
                                 ).then_inc(high_set, 1)

            for t in range(NT):
                if t == NT - 1:
                    act.wait_ge(mixed, NT)
                    s.activation(den[:], den[:], ACT.Copy).then_inc(high_used, 2)
                    high_part(0, 0, 0, True)
                act.wait_ge(h_set, t + 1)
                s.activation(normed[:, t, :], hx[:, t, :], ACT.Square, accum_out=sq[:, t:t + 1]).then_inc(squared, 1)
                act.wait_ge(var_set, 6 + t)
                s.activation(rstd[:, t:t + 1], rstd[:, t:t + 1], ACT.Sqrt).then_inc(rooted, 1)
            act.dma_start(sums[0:SEQ, :].rearrange("(t p) d -> p t d", p=P), hx[:]).then_inc(sums_set, 16)
            act.wait_ge(xn_set, 9)
            act.dma_start(normed_rows.rearrange("(t p) d -> p t d", p=P), normed[:, :, :]).then_inc(normed_stored, 16)
            high_part(1, 0, 1, True)
            act.wait_ge(top_set, 1)
            s.activation(top_e[:], top_e[:], ACT.Exp).then_inc(top_exp, 1)

            s.activation(sink_e[:], sink_e[:], ACT.Copy).then_inc(y_scaled, 1)

            act.wait_ge(rounds_set, 1)
            rounds = act.value_load(rounds_i[0:1, 0:1], min_val=1, max_val=ROUNDS)
            with act.Fori(0, rounds) as r:
                with act.Fori(0, BODIES) as b:
                    for j in range(UNROLL):
                        A = r * NE + b * UNROLL + j

                        def sigmoid(h):
                            act.wait_ge(gate_capped, A * 2 + (h + 1))
                            s.activation(glu_t[:, h * COLS:(h + 1) * COLS], gate_t[:, h * COLS:(h + 1) * COLS],
                                         ACT.Sigmoid, scale=ALPHA).then_inc(sigmoids, 1)

                        def actT_out(h):
                            act.wait_ge(act_T, A * 2 + (h + 1))
                            for dst in (actT, act_high):
                                i = s.activation(dst[:, 4 * h:4 * h + 4, :],
                                                 bank[6 + h][:, 0:4 * CAP].rearrange("p (k n) -> p k n", k=4), ACT.Copy)
                            i.then_inc(actT_set, 1)

                        high_part(2, A, j % 2)
                        sigmoid(0)
                        high_part(3, A, (j + 1) % 2)
                        high_part(4, A, j % 2)
                        actT_out(0)
                        sigmoid(1)
                        high_part(0, A + 1, (j + 1) % 2)
                        actT_out(1)
                        for i, h in enumerate((1, 0)):
                            act.wait_ge(down_ready, A * 2 + (i + 1))
                            if i == 0:
                                act.wait_ge(sums_landed, A * 16 + FIRST_SUMS - 16)
                            s.activation(y_rows[j % 2][:, h * COLS:(h + 1) * COLS], bank[4 + h][0:CAP, :], ACT.Copy,
                                         scale=gate_c[0:CAP, j:j + 1]).then_inc(y_scaled, 1)
                        high_part(1, A + 1, j % 2)

            s.activation(mx[:, 0:1], iota_cap[:, 0:1], ACT.Sqrt)
            for t in range(NT):
                act.wait_ge(final_in[t], 16)
                s.activation(normed[:, t, :], hx[:, t, :], ACT.Square, accum_out=sq[:, t:t + 1]).then_inc(squared, 1)
                act.wait_ge(var_set, 10 + t)
                s.activation(rstd[:, t:t + 1], rstd[:, t:t + 1], ACT.Sqrt).then_inc(rooted, 1)

        @block.vector
        def _(dve):
            v = nc.vector
            seq = [0]

            def then(ins):
                seq[0] += 1
                ins.then_inc(dve_seq, 1)
                dve.wait_ge(dve_seq, seq[0])

            def norm(t, done, src, dst, n=P, weight=None):
                dve.wait_ge(squared, done + 1)
                v.tensor_scalar(rstd[0:n, t:t + 1], sq[0:n, t:t + 1], 1.0 / D, EPS, ALU.mult, ALU.add).then_inc(var_set, 1)
                dve.wait_ge(rooted, done + 1)
                then(v.reciprocal(rstd[0:n, t:t + 1], rstd[0:n, t:t + 1]))
                if weight is not None:
                    v.scalar_tensor_tensor(out=dst, in0=src, scalar=rstd[0:n, t:t + 1], in1=weight, op0=ALU.mult,
                                           op1=ALU.mult).then_inc(out_set, 1)
                else:
                    v.tensor_scalar(dst, src, rstd[0:n, t:t + 1], None, ALU.mult).then_inc(xn_set, 1)

            v.memset(block_of[:], 0.0)
            then(v.memset(unseen[:], 0.0))
            for q in (0, 64):
                v.memset(block_of[q:q + 1, 0:64], 1.0)
                v.memset(block_of[q + 32:q + 33, 64:128], 1.0)
                v.memset(unseen[q:q + 1, :, PREV + 64:KEYS], NEG)
                v.memset(unseen[q + 32:q + 33, :, 0:64], NEG)
                v.memset(unseen[q:q + 1, 0, 0:64], NEG)
            dve.wait_ge(vecs_T, 1)
            v.tensor_copy(vec[:, 0:29], bank[7][:, 0:29]).then_inc(vecs_set, 1)
            dve.wait_ge(vecs_set, 1)

            def u_out(t):
                for h in range(2):
                    dve.wait_ge(u_T, 2 * t + h + 1)
                    v.tensor_tensor(uT[:, 4 * h:4 * h + 4, t * P:(t + 1) * P],
                                    bank[(2 * t + h) % 4][:].rearrange("p (k n) -> p k n", k=4),
                                    spread(col(VG_MIX + 4 * h, 4), P), ALU.mult).then_inc(u_set, 1)

            for t in range(NT):
                norm(t, t, hx[:, t, :], xn[:, t, :])
                if t:
                    u_out(t - 1)
            u_out(NT - 1)
            norm(NT, NT, meta_x, meta_n, META)
            dve.wait_ge(u_T, 2 * NT + 1)
            v.tensor_tensor(uT_meta, bank[4][:, 0:KC * META].rearrange("p (k n) -> p k n", k=KC),
                            spread(col(VG_MIX, KC), META), ALU.mult).then_inc(u_set, 1)

            def split_low_part(i):
                high, whole, low = parts_of[i]
                for p in range(2):
                    dve.wait_ge(split_high, 2 * i + p + 1)
                    v.tensor_tensor(half_unit(low, p), half_unit(whole, p), half_unit(high, p), ALU.subtract
                                    ).then_inc(split_low, 1)

            split_low_part(0)
            split_low_part(1)

            v.memset(k_prev[:, 0, 0:64], 0.0)
            v.memset(v_prev[0:64, 0, :], 0.0)
            dve.wait_ge(proj_set, 2)
            for m in range(1, NT):
                v.tensor_copy(k_prev[:, m, 0:64], kT[:, m * P - 64:m * P])
                v.tensor_copy(k_prev[:, m, 64:PREV], k_prev[:, 0, 64:PREV])
            dve.wait_ge(proj, 3)
            dve.wait_ge(consts_in, 16 * 5)
            then(v.tensor_tensor(v_own, bank[6][:].rearrange("p (m n) -> p m n", m=NT),
                                 bv.unsqueeze(1).to_broadcast([P, NT, P]), ALU.add))
            for m in range(NT):
                v.tensor_tensor(v_prev[64:PREV, m, :], bank[5][0:META, 128:256], bv[0:META, :], ALU.add)
                if m:
                    i = v.tensor_copy(v_prev[0:64, m, :], v_own[64:128, m - 1, :])
            i.then_inc(v_set, 1)
            split_low_part(2)

            def pool_windows(g):
                dve.wait_ge(p_set, g + 1)
                if g:
                    dve.wait_ge(diff_set, g)
                src, w, lo = pT[:, g, :], 1, 0
                for i in range(g + 1):
                    dst = wsum[i % 2]
                    then(v.tensor_tensor(dst[:, lo + w:L], src[:, lo + w:L], src[:, lo:L - w], ALU.add))
                    src, lo, w = dst, lo + w, 2 * w
                v.scalar_tensor_tensor(out=diffT[:, g, :], in0=src[:, META:L], scalar=1.0 / POOL_WINDOWS[g],
                                       in1=pT[:, g, META:L], op0=ALU.mult, op1=ALU.subtract).then_inc(diff_set, 1)

            def mix_out_of(m):
                dve.wait_ge(attended, m + 1)
                v.tensor_copy(mixT[:, 0:4, m * P:(m + 1) * P], bank[7][:].rearrange("p (c q) -> p c q", c=4)
                              ).then_inc(mix_set, 1)

            for m in range(NT):
                dve.wait_ge(scored, m + 1)
                if m:
                    dve.wait_ge(exp_set, 2 * m)
                for g in range(2):
                    heads = slice(HALF * g, HALF * g + HALF)
                    for i in range(2 * g, 2 * g + 2):
                        ins = v.tensor_reduce(mx[:, 2 * i:2 * i + 2],
                                              bank[i][:, 0:2 * KEYS].rearrange("p (h k) -> p h k", h=2), AX.X, ALU.max)
                    then(ins)
                    then(v.scalar_tensor_tensor(out=mx[:, heads], in0=mx[:, heads], scalar=SCALE, in1=sinks[:, heads],
                                                op0=ALU.mult, op1=ALU.max))
                    v.tensor_tensor(sink_e[:, heads], sinks[:, heads], mx[:, heads], ALU.subtract)
                    v.tensor_scalar(negm[:, heads], mx[:, heads], -1.0, None, ALU.mult).then_inc(max_set, 1)
                if m:
                    mix_out_of(m - 1)
                for g in range(2):
                    heads = slice(HALF * g, HALF * g + HALF)
                    dve.wait_ge(exp_set, 2 * m + g + 1)
                    then(v.tensor_tensor(den[:, heads], den[:, heads], sink_e[:, heads], ALU.add))
                    then(v.reciprocal(den[:, heads], den[:, heads]))
                    v.tensor_tensor(probs[:, heads, :], probs[:, heads, :], spread(den[:, heads], KEYS), ALU.mult
                                    ).then_inc(probs_set, 1)
                for g in range(2):
                    dve.wait_ge(probs_T, 2 * m + g + 1)
                    v.tensor_copy(probsT_prev[g], bank[5 if g == 0 else 0][0:PREV, :].rearrange("p (h q) -> p h q", h=4)
                                  ).then_inc(probsT_set[g], 1)
                if m and m < NT - 1:
                    pool_windows(m - 1)

            mix_out_of(NT - 1)
            pool_windows(NG - 2)
            pool_windows(NG - 1)

            def low_part(u, A, buffer, pieces=(0, 1)):
                for p in pieces:
                    dve.wait_ge(high_set, A * (2 * SPLIT) + (2 * u + p + 1))
                    v.tensor_tensor(half_unit(ring_low[u], p), half_unit(ring[u], p), half_unit(high_of[buffer], p),
                                    ALU.subtract).then_inc(low_set, 1)

            def residual(t):
                dve.wait_ge(mixed, t + 1)
                for h in range(2):
                    i = v.tensor_tensor(hx[:, t, h * 512:(h + 1) * 512], bank[2 * t + h][:],
                                        hx[:, t, h * 512:(h + 1) * 512], ALU.add)
                i.then_inc(h_set, 1)

            def f_out(t):
                for h in range(2):
                    dve.wait_ge(f_T, 2 * t + h + 1)
                    v.tensor_tensor(fT[:, 4 * h:4 * h + 4, t * P:(t + 1) * P],
                                    bank[2 * t + h][:].rearrange("p (k n) -> p k n", k=4),
                                    spread(col(VG_FFN + 4 * h, 4), P), ALU.mult).then_inc(f_set, 1)

            def top4(t):
                dve.wait_ge(routed, t + 1)
                then(v.scalar_tensor_tensor(out=logits[:, t, :], in0=bank[2 * t][:, 0:NE], scalar=rstd[:, t:t + 1],
                                            in1=b_router[:], op0=ALU.mult, op1=ALU.add))
                then(v.max(top[:, t, :], logits[:, t, :]))
                then(v.max_index(top_at[:, t, :], top[:, t, :], logits[:, t, :]))

            for t in range(NT):
                residual(t)
                if t < NT - 1:
                    norm(t, NT + 1 + t, hx[:, t, :], normed[:, t, :])
                if t == 1:
                    dve.wait_ge(parts_set, 1)
                if t:
                    f_out(t - 1)
                    if t < NT - 1:
                        top4(t - 1)
            f_out(NT - 1)
            norm(NT - 1, NT + 1 + NT - 1, hx[:, NT - 1, :], normed[:, NT - 1, :])
            low_part(0, 0, 0, (0,))
            top4(NT - 2)
            low_part(0, 0, 0, (1,))
            top4(NT - 1)
            v.tensor_tensor(top_e[:], top[:, :, 0:TOPK], top[:, :, 0:1].to_broadcast([P, NT, TOPK]),
                            ALU.subtract).then_inc(top_set, 1)
            then(v.tensor_copy(top_f[:], top_at[:]))

            def over_experts(ap):
                return ap.unsqueeze(3).to_broadcast([P, NT, TOPK, NE])

            then(v.tensor_tensor(chosen, iota_exp[:].unsqueeze(1).unsqueeze(1).to_broadcast([P, NT, TOPK, NE]),
                                 over_experts(top_f[:, :, 0:TOPK]), ALU.is_equal))
            then(v.tensor_reduce(mask[:], chosen.rearrange("p t k e -> p t e k"), AX.X, ALU.add))
            v.tensor_copy(mask_b[:], mask[:]).then_inc(mask_set, 1)
            dve.wait_ge(mask_set, 1)
            then(v.tensor_scalar(mask[:], mask[:], FAR, CAP - FAR, ALU.mult, ALU.add))
            dve.wait_ge(top_exp, 1)
            then(v.tensor_reduce(top_s[:], top_e[:], AX.X, ALU.add))
            then(v.reciprocal(top_s[:], top_s[:]))
            then(v.tensor_tensor(top_e[:], top_e[:], spread(top_s[:], TOPK), ALU.mult))
            then(v.tensor_tensor(chosen_g, chosen, over_experts(top_e[:]), ALU.mult))
            then(v.tensor_reduce(gates[:], chosen_g.rearrange("p t k e -> p t e k"), AX.X, ALU.add))
            parts = gate_parts[:].rearrange("p t (e c) -> p t e c", c=3)
            v.memset(gate_parts[:, :, 3 * NE:3 * NEP], 0.0)
            for c in range(3):
                then(v.tensor_copy(parts[:, :, 0:NE, c], gates[:]))
                if c < 2:
                    then(v.tensor_tensor(gates[:], gates[:], parts[:, :, 0:NE, c], ALU.subtract))
            dve.wait_ge(ranked, 1)
            v.tensor_tensor(ranks[:, :, 0:NE], bank[2][:, 0:NT * NE].rearrange("p (t e) -> p t e", t=NT),
                            mask[:], ALU.add)
            then(v.tensor_reduce(count[:], bank[3][:, 0:NE], AX.X, ALU.max))
            then(v.tensor_scalar(over[:], steps[:], count[:], None, ALU.is_lt))
            then(v.tensor_reduce(rounds_f[:], over[:], AX.X, ALU.add))
            v.tensor_copy(rounds_i[:], rounds_f[:]).then_inc(rounds_set, 1)
            dve.wait_ge(rounds_set, 1)
            rounds = dve.value_load(rounds_i[0:1, 0:1], min_val=1, max_val=ROUNDS)

            def mark(e):
                v.tensor_tensor(hot[:], iota_cap[:].unsqueeze(1).to_broadcast([P, NT, CAP]),
                                ranks[:, :, bass.ds(e, 1)].to_broadcast([P, NT, CAP]), ALU.is_equal)
                v.tensor_copy(place_in[:, :, 2:5], gate_parts[:, :, bass.ds(e * 3, 3)]).then_inc(hot_set, 1)

            def places(j, I):
                dve.wait_ge(place_ready, I + 1)
                j = j % UNROLL
                src = bank[7][0:CAP, 4 * CAP:4 * CAP + 6]
                v.tensor_reduce(token_f[0:CAP], src[:, 0:2], AX.X, ALU.add)
                v.tensor_reduce(gate_c[0:CAP, j:j + 1], src[:, 2:5], AX.X, ALU.add)
                v.tensor_scalar(to_f[0:CAP], src[:, 5:6], spare[0:CAP, 1:2], spare[0:CAP, 0:1],
                                ALU.mult, ALU.add).then_inc(ranks_moved, 1)

            def places_end(j, n):
                dve.wait_ge(ranks_moved, n)
                j = j % UNROLL
                v.tensor_copy(from_row[0:CAP, j:j + 1], token_f[0:CAP])
                v.tensor_tensor(to_row[0:CAP, j:j + 1], to_f[0:CAP], token_f[0:CAP], ALU.add).then_inc(place_set, 1)

            def x_out(n):
                for h in range(2):
                    k = slice(4 * h, 4 * h + 4)
                    dve.wait_ge(x_T, n + h + 1)
                    v.tensor_tensor(x_f[:, k, :], bank[7 - h][:, 0:4 * CAP].rearrange("p (k n) -> p k n", k=4),
                                    spread(col(VG_FFN + 4 * h, 4), CAP), ALU.mult).then_inc(xf_set, 1)
                for h in range(2):
                    k = slice(4 * h, 4 * h + 4)
                    dve.wait_ge(xf_set, n + h + 1)
                    v.tensor_copy(x_high[:, k, :], x_f[:, k, :]).then_inc(xh_set, 1)
                for h in range(2):
                    k = slice(4 * h, 4 * h + 4)
                    dve.wait_ge(xh_set, n + h + 1)
                    v.tensor_tensor(x_low[:, k, :], x_f[:, k, :], x_high[:, k, :], ALU.subtract
                                    ).then_inc(xT_set, 1)

            dve.wait_ge(normed_stored, 16)
            with dve.Fori(0, rounds) as r:
                v.tensor_scalar(ranks[:], ranks[:], -float(CAP), None, ALU.add).then_inc(ranks_moved, 1)
                dve.wait_ge(ranks_moved, r * (NEP + 1) + 1)
                dve.wait_ge(sums_landed, r * (16 * NE) + FIRST_SUMS)
                for j in range(AHEAD):
                    mark(j)
                    places(j, r * NEP + j)
                    places_end(j, r * (NEP + 1) + (2 + j))
                x_out(r * (2 * (NE + 1)))
                with dve.Fori(0, BODIES) as b:
                    for j in range(UNROLL):
                        A = r * NE + b * UNROLL + j

                        def cap_gate(h):
                            dve.wait_ge(gate_ready, A * 2 + (h + 1))
                            v.tensor_scalar(gate_t[:, h * COLS:(h + 1) * COLS], bank[2 * h][0:CAP, :], LIMIT, None,
                                            ALU.min).then_inc(gate_capped, 1)

                        def activate(h):
                            c = slice(h * COLS, (h + 1) * COLS)
                            dve.wait_ge(sigmoids, A * 2 + (h + 1))
                            v.tensor_tensor(glu_t[:, c], gate_t[:, c], glu_t[:, c], ALU.mult).then_inc(glu_set, 1)
                            dve.wait_ge(up_ready, A * 2 + (h + 1))
                            v.tensor_scalar(up_t[:, c], bank[2 * h + 1][0:CAP, :], LIMIT + 1.0, None, ALU.min
                                            ).then_inc(up_capped, 1)
                            dve.wait_ge(up_capped, A * 2 + (h + 1))
                            v.scalar_tensor_tensor(out=act_t[:, c], in0=up_t[:, c], scalar=1.0 - LIMIT,
                                                   in1=glu_t[:, c], op0=ALU.max, op1=ALU.mult).then_inc(act_set, 1)

                        def act_rest(h):
                            dve.wait_ge(actT_set, A * 2 + (h + 1))
                            k = slice(4 * h, 4 * h + 4)
                            v.tensor_tensor(act_low[:, k, :], actT[:, k, :], act_high[:, k, :], ALU.subtract
                                            ).then_inc(act_low_set, 1)

                        mark(b * UNROLL + (j + AHEAD))
                        cap_gate(0)
                        low_part(2, A, j % 2)
                        activate(0)
                        low_part(3, A, (j + 1) % 2)
                        dve.wait_ge(sums_landed, A * 16 + FIRST_SUMS - 16)
                        places(j + AHEAD, r * NEP + b * UNROLL + (j + AHEAD))
                        places_end(j + AHEAD, r * (NEP + 1) + b * UNROLL + (j + AHEAD + 2))
                        cap_gate(1)
                        act_rest(0)
                        low_part(4, A, j % 2, (0,))
                        activate(1)
                        x_out((r * (NE + 1) + b * UNROLL + (j + 1)) * 2)
                        low_part(4, A, j % 2, (1,))
                        act_rest(1)
                        low_part(0, A + 1, (j + 1) % 2)
                        low_part(1, A + 1, j % 2)

            for t in range(NT):
                dve.wait_ge(final_in[t], 16)
                if t == 0:
                    dve.wait_ge(g_final_in, 16)
                norm(t, 2 * NT + 1 + t, hx[:, t, :], normed[:, t, :], weight=g_final)

        @block.tensor
        def _(pe):
            mm = nc.tensor.matmul

            def tr(dst, src):
                return mm(dst, src, ident[0:src.shape[0], 0:src.shape[0]], start=True, stop=True, is_transpose=True)

            pe.wait_ge(consts_set, 2)
            pe.wait_ge(vec_in, 16 * 5)
            tr(bank[7][:, 0:29], vec_rows[0:29, :]).then_inc(vecs_T, 1)
            for t in range(NT):
                pe.wait_ge(xn_set, t + 1)
                if t >= 2:
                    pe.wait_ge(u_set, 2 * (t - 1))
                for h in range(2):
                    for k in range(4):
                        i = tr(bank[(2 * t + h) % 4][:, k * P:(k + 1) * P], xn[:, t, (4 * h + k) * P:(4 * h + k + 1) * P])
                    i.then_inc(u_T, 1)
            pe.wait_ge(u_set, 2 * NT)
            pe.wait_ge(vecs_set, 1)

            def project(dst, lhs, rhs):
                for k in range(KC):
                    i = mm(dst, lhs(k), rhs(k), start=k == 0, stop=k == KC - 1)
                return i

            def project_split(dst, w, c):
                for k in range(KC):
                    for of_w, of_u in ((0, 0), (1, 0), (0, 1)):
                        i = mm(dst, w[of_w][:, k, c * P:(c + 1) * P], u_parts[of_u][:, k, :],
                               start=k == 0 and of_w + of_u == 0, stop=k == KC - 1 and of_u == 1)
                return i

            pe.wait_ge(wkv_in, 16)
            project(bank[0][:, 0:SEQ], lambda k: wkv[:, k, 0:128], lambda k: uT[:, k, :]).then_inc(proj, 1)
            pe.wait_ge(xn_set, NT + 1)
            for k in range(KC):
                i = tr(bank[4][:, k * META:(k + 1) * META], meta_n[:, k * P:(k + 1) * P])
            i.then_inc(u_T, 1)
            pe.wait_ge(u_set, 2 * NT + 1)
            pe.wait_ge(wp_in, 16)
            project(bank[5][:, 0:META], lambda k: wkv[:, k, 0:128], lambda k: uT_meta[:, k, :])
            for c in range(NG):
                project(bank[5][:, META * (1 + c):META * (2 + c)], lambda k: wp[:, k, c * P:(c + 1) * P],
                        lambda k: uT_meta[:, k, :])
            project(bank[5][0:META, 128:256], lambda k: uT_meta[:, k, :], lambda k: wkv[:, k, 128:256]).then_inc(proj, 1)
            for m in range(NT):
                i = project(bank[6][:, m * P:(m + 1) * P], lambda k: uT[:, k, m * P:(m + 1) * P],
                            lambda k: wkv[:, k, 128:256])
            i.then_inc(proj, 1)
            pe.wait_ge(split_low, 4)
            for c in range(4):
                project_split(bank[1 + c][:], wq_parts, c).then_inc(proj, 1)

            pe.wait_ge(proj_set, 6)
            pe.wait_ge(v_set, 1)
            def scores(m):
                if m:
                    pe.wait_ge(probsT_set[1], 2 * m)
                for h in range(HEADS):
                    g, c = divmod(h, HALF)
                    rows = slice(64 * g, 64 * g + 64)
                    dst = bank[h // 2][:, (h % 2) * KEYS:(h % 2 + 1) * KEYS]
                    q = qT[rows, c, m * P:(m + 1) * P]
                    mm(dst, block_of[rows, :], unseen[rows, min(m, 1), :], start=True, stop=False)
                    mm(dst[:, 0:PREV], q, k_prev[rows, m, :], start=False, stop=False)
                    i = mm(dst[:, PREV:KEYS], q, kT[rows, m * P:(m + 1) * P], start=False, stop=True)
                i.then_inc(scored, 1)

            def attend(m, g):
                pe.wait_ge(probsT_set[g], 2 * m + 2)
                for c in range(HALF):
                    dst = bank[7][64 * g:64 * g + 64, c * P:(c + 1) * P]
                    mm(dst, v_prev[0:PREV, m, 64 * g:64 * g + 64], probsT_prev[g][:, c, :], start=True, stop=False)
                    i = mm(dst, v_own[:, m, 64 * g:64 * g + 64], probsT_own[g][:, c, :], start=False, stop=True)
                return i

            scores(0)
            for m in range(NT):
                pe.wait_ge(split_low, 6)
                if m:
                    pe.wait_ge(p_set, m)
                project_split(bank[4][:], wp_parts, m).then_inc(proj, 1)
                for g in range(2):
                    pe.wait_ge(probs_set, 2 * m + g + 1)
                    prev, own = (bank[5], bank[6]) if g == 0 else (bank[0], bank[1])
                    for c in range(HALF):
                        tr(prev[0:PREV, c * P:(c + 1) * P], probs[:, HALF * g + c, 0:PREV])
                        i = tr(own[:, c * P:(c + 1) * P], probs[:, HALF * g + c, PREV:KEYS])
                    i.then_inc(probs_T, 1)
                if m:
                    pe.wait_ge(mix_set, m)
                attend(m, 0)
                if m < NT - 1:
                    scores(m + 1)
                attend(m, 1).then_inc(attended, 1)

            def pooling(g):
                pe.wait_ge(diff_set, g + 1)
                mm(bank[2 + g][:], w_pool[:, g, :], diffT[:, g, :], start=True, stop=True).then_inc(pooled, 1)

            for g in range(2):
                pooling(g)

            pe.wait_ge(mix_set, NT)

            def logits_of(t):
                pe.wait_ge(h_set, t + 1)
                for h in range(2):
                    for k in range(4):
                        i = tr(bank[2 * t + h][:, k * P:(k + 1) * P],
                               hx[:, t, (4 * h + k) * P:(4 * h + k + 1) * P])
                    i.then_inc(f_T, 1)

            def route(t):
                pe.wait_ge(f_set, 2 * t + 2)
                project(bank[2 * t][:, 0:NE], lambda k: fT[:, k, t * P:(t + 1) * P],
                        lambda k: w_router[:, k, :]).then_inc(routed, 1)

            def mix_out(t, h, chunks):
                for k in chunks:
                    i = mm(bank[2 * t + h][:], mixT[:, k, t * P:(t + 1) * P], wout[h][:, k, :],
                           start=k == 0, stop=k == KC - 1)
                return i

            for t in range(NT):
                for chunks in (range(0, 4), range(4, KC)):
                    if t == 0 and chunks[0]:
                        for g in range(2, NG):
                            pooling(g)
                        pe.wait_ge(pooled_set, NG)
                    for h in range(2):
                        if t == 0 and not chunks[0]:
                            pe.wait_ge(wout_in[h], 16)
                        i = mix_out(t, h, chunks)
                i.then_inc(mixed, 1)
                if t >= 1:
                    logits_of(t - 1)
                if t >= 2:
                    route(t - 2)
            logits_of(NT - 1)
            route(NT - 2)
            route(NT - 1)

            pe.wait_ge(mask_set, 1)
            for t in range(NT):
                dst = bank[2][:, t * NE:(t + 1) * NE]
                for q in range(t):
                    mm(dst, ones[:], mask_b[:, q, :], start=q == 0, stop=False)
                mm(dst, earlier[:], mask_b[:, t, :], start=t == 0, stop=True)
            for q in range(NT):
                i = mm(bank[3][:, 0:NE], ones[:], mask_b[:, q, :], start=q == 0, stop=q == NT - 1)
            i.then_inc(ranked, 1)

            pe.wait_ge(rounds_set, 1)
            rounds = pe.value_load(rounds_i[0:1, 0:1], min_val=1, max_val=ROUNDS)

            def find(I):
                pe.wait_ge(hot_set, I + 1)
                for t in range(NT):
                    i = mm(bank[7][0:CAP, 4 * CAP:4 * CAP + 6], hot[:, t, :], place_in[:, t, :],
                           start=t == 0, stop=t == NT - 1)
                i.then_inc(place_ready, 1)

            def x_transpose(j, G, I, first=None):
                pe.wait_ge(gathered[j % 2], G * 16 + 16)
                pe.wait_ge(place_set, I)
                for h in range(2):
                    if h and first is not None:
                        pe.wait_ge(actT_set, first)
                    for k in range(4):
                        i = tr(bank[7 - h][:, k * CAP:(k + 1) * CAP], x_rows[j % 2][:, (4 * h + k) * P:(4 * h + k + 1) * P])
                    i.then_inc(x_T, 1)

            per_round = NEP // 2
            with pe.Fori(0, rounds) as r:
                find(r * NEP)
                pe.wait_ge(place_set, r * NEP + 1)
                find(r * NEP + 1)
                x_transpose(0, r * per_round, r * NEP + 2)
                with pe.Fori(0, BODIES) as b:
                    for j in range(UNROLL):
                        A = r * NE + b * UNROLL + j
                        X = r * (NE + 1) + b * UNROLL + j
                        I = r * NEP + b * UNROLL + (j + AHEAD)

                        def bias(dst, kind, half):
                            c = kind * D + half * COLS
                            mm(dst, bias_row[:, j % 2, :], bias_parts[:, c:c + COLS], start=True, stop=False)

                        def act_transpose(h):
                            pe.wait_ge(act_set, A * 2 + (h + 1))
                            for k in range(4):
                                i = tr(bank[6 + h][:, k * CAP:(k + 1) * CAP],
                                       act_t[:, (4 * h + k) * P:(4 * h + k + 1) * P])
                            i.then_inc(act_T, 1)

                        def down(half):
                            for f in range(4 * half, 4 * half + 4):
                                i = mm(bank[5][0:CAP, :], actT[:, f, :], slot[5][:, f, :], start=False, stop=f == KC - 1)
                            if half:
                                i.then_inc(down_ready, 1)

                        def split_half(dst, u, p, high, low, last):
                            wh = high_of[(j + u) % 2][:].rearrange("p (k n) -> p k n", k=KC)
                            wl = ring_low[u][:].rearrange("p (k n) -> p k n", k=KC)
                            pe.wait_ge(high_set, A * (2 * SPLIT) + (2 * u + p + 1))
                            for k in range(4 * p, 4 * p + 4):
                                mm(dst, high[:, k, :], wh[:, k, :], start=False, stop=False)
                                i = mm(dst, low[:, k, :], wh[:, k, :], start=False, stop=False)
                            if p:
                                i.then_inc(high_used, 1)
                            pe.wait_ge(low_set, A * (2 * SPLIT) + (2 * u + p + 1))
                            for k in range(4 * p, 4 * p + 4):
                                i = mm(dst, high[:, k, :], wl[:, k, :], start=False, stop=k == KC - 1)
                            if p:
                                i.then_inc(last, 1)

                        pe.wait_ge(bias_set, X + 1)
                        pe.wait_ge(xT_set, X * 2 + 2)
                        for u in range(4):
                            half, kind = divmod(u, 2)
                            dst = bank[u][0:CAP, :]
                            bias(dst, kind, half)
                            for p in range(2):
                                split_half(dst, u, p, x_high, x_low, up_ready if kind else gate_ready)
                            if u == 1:
                                find(I)
                            if u == 2:
                                act_transpose(0)
                        x_transpose(j + 1, r * per_round + b * 2 + (j + 1) // 2, I + 1, A * 2 + 1)
                        pe.wait_ge(y_scaled, A * 2 + 1)
                        bias(bank[4][0:CAP, :], 2, 0)
                        pe.wait_ge(act_low_set, A * 2 + 1)
                        split_half(bank[4][0:CAP, :], 4, 0, act_high, act_low, None)
                        pe.wait_ge(xf_set, X * 2 + 3)
                        act_transpose(1)
                        pe.wait_ge(weights_in[5], A * 16 + 16)
                        bias(bank[5][0:CAP, :], 2, 1)
                        down(0)
                        pe.wait_ge(actT_set, A * 2 + 2)
                        down(1)
                        pe.wait_ge(act_low_set, A * 2 + 2)
                        split_half(bank[4][0:CAP, :], 4, 1, act_high, act_low, down_ready)
                pe.wait_ge(gathered[1], (r * per_round + per_round) * 16)
                pe.wait_ge(xT_set, (r + 1) * (2 * (NE + 1)))


_SHAPE = (1, SEQ, D)


def kernel(**inputs):
    import numpy as _np
    import concourse.bacc as _bacc
    from concourse import mybir as _mybir
    from concourse.bass_utils import run_bass_kernel_spmd as _run

    nc = _bacc.Bacc("TRN2", target_bir_lowering=False, num_devices=1)
    def pairs(x, axis):
        at = [2 * h + g for g in range(2) for h in range(HALF)]
        order = _np.argsort(at)
        parts = _np.split(_np.asarray(x), [HEADS * HD], axis=axis)
        heads = _np.split(parts[0], HEADS, axis=axis)
        return _np.concatenate([heads[i] for i in order] + [parts[1]], axis=axis)

    inputs = dict(inputs, w_in=pairs(inputs["w_in"], 2), b_in=pairs(inputs["b_in"], 1),
                  w_out=pairs(inputs["w_out"], 1))
    arrays, args = {}, {}
    for name, x in inputs.items():
        x = _np.ascontiguousarray(x)
        arrays[f"in_{name}"] = x
        args[name] = nc.dram_tensor(f"in_{name}", x.shape, _mybir.dt.from_np(x.dtype), kind="ExternalInput").ap()
    out = nc.dram_tensor("out_0", _SHAPE, _mybir.dt.float32, kind="ExternalOutput").ap()
    build(nc, args, out)
    r = _run(nc, [arrays], core_ids=[0])
    return r.results[0]["out_0"]
```
